# Optimizing a Trainium2 kernel written in Bass

```python
import jax, jax.numpy as jnp
from jax import lax
import numpy as np

D_MODEL = 1024
BATCH = 1
SEQ = 512
DEPTH = 1
DEC_BATCH = 1
DEC_SEQ = 32
PAST_LEN = 1024

CHUNK = 64
D_MIX = D_MODEL
D_MLSTM = D_MIX // 2
D_RET = D_MIX - D_MLSTM
H_M = 4
H_R = 4
DH_M = D_MLSTM // H_M
DH_R = D_RET // H_R
D_FF = ((8 * D_MODEL // 3 + 255) // 256) * 256
D_IN = 4 * D_MLSTM + 4 * D_RET + 2 * H_M
ROPE_BASE = 10000.0
EPS = 1e-6
GN_EPS = 1e-5
LOG_GAMMA = np.log(1.0 - 2.0 ** (-5.0 - np.arange(H_R))).astype(np.float32)

kernel_name = "hymba_mlstm_retention_macaron_stream_step"

def rms_norm(x, g):
    xf = x.astype(jnp.float32)
    y = xf * lax.rsqrt(jnp.mean(xf * xf, axis=-1, keepdims=True) + EPS)
    return (y * g.astype(jnp.float32)).astype(x.dtype)

def swiglu(x, wg, wu, wd):
    return (jax.nn.silu(x @ wg) * (x @ wu)) @ wd

def heads(a, n_heads):
    b, s, _ = a.shape
    return a.reshape(b, s, n_heads, -1).transpose(0, 2, 1, 3)

def head_group_norm(h, g):
    mu = jnp.mean(h, axis=-1, keepdims=True)
    var = jnp.mean(jnp.square(h - mu), axis=-1, keepdims=True)
    hn = (h - mu) * lax.rsqrt(var + GN_EPS)
    b, nh, s, d = h.shape
    return hn.transpose(0, 2, 1, 3).reshape(b, s, nh * d) * g.astype(jnp.float32)

def rope(x, pos):
    half = x.shape[-1] // 2
    inv = ROPE_BASE ** (-jnp.arange(half, dtype=jnp.float32) / half)
    ang = pos.astype(jnp.float32)[:, None] * inv[None, :]
    cos, sin = jnp.cos(ang), jnp.sin(ang)
    x1, x2 = x[..., :half], x[..., half:]
    return jnp.concatenate([x1 * cos - x2 * sin, x1 * sin + x2 * cos], axis=-1)

def mlstm_chunk(carry, inp):
    C, n, m = carry
    q, k, v, ig, lf = inp
    L = q.shape[2]
    b = jnp.cumsum(lf, axis=-1)
    causal = jnp.tril(jnp.ones((L, L), dtype=bool))
    logw = jnp.where(causal, b[..., :, None] - b[..., None, :] + ig[..., None, :], -jnp.inf)
    log_prev = b + m[..., None]
    m_t = jnp.maximum(log_prev, jnp.max(logw, axis=-1))
    w = jnp.exp(logw - m_t[..., None])
    a = jnp.exp(log_prev - m_t)
    s = jnp.einsum('bhtd,bhsd->bhts', q, k) * w
    num = a[..., None] * jnp.einsum('bhtd,bhde->bhte', q, C) + jnp.einsum('bhts,bhse->bhte', s, v)
    den = a * jnp.einsum('bhtd,bhd->bht', q, n) + jnp.sum(s, axis=-1)
    h = num / jnp.maximum(jnp.abs(den), jnp.exp(-m_t))[..., None]
    m_last = m_t[..., -1]
    w_last = jnp.exp(b[..., -1:] - b + ig - m_last[..., None])
    a_last = jnp.exp(b[..., -1] + m - m_last)
    C_new = a_last[..., None, None] * C + jnp.einsum('bhs,bhsd,bhse->bhde', w_last, k, v)
    n_new = a_last[..., None] * n + jnp.einsum('bhs,bhsd->bhd', w_last, k)
    return (C_new, n_new, m_last), h

def retention_chunk(R, inp):
    q, k, v = inp
    L = q.shape[2]
    lg = jnp.asarray(LOG_GAMMA)
    idx = jnp.arange(L, dtype=jnp.float32)
    diff = idx[:, None] - idx[None, :]
    decay = jnp.where(diff >= 0, jnp.exp(lg[:, None, None] * jnp.maximum(diff, 0.0)), 0.0)
    scores = jnp.einsum('bhtd,bhsd->bhts', q, k) * decay
    inner = jnp.einsum('bhts,bhse->bhte', scores, v)
    cross = jnp.exp(lg[:, None] * (idx + 1.0))
    out = inner + cross[:, :, None] * jnp.einsum('bhtd,bhde->bhte', q, R)
    tail = jnp.exp(lg[:, None] * (L - 1.0 - idx))
    R_new = jnp.exp(lg * L)[:, None, None] * R + jnp.einsum('hs,bhsd,bhse->bhde', tail, k, v)
    return R_new, out

def chunked_scan(step, state, seqs, L):
    def to_blocks(a):
        bsz, nh, s = a.shape[:3]
        return jnp.moveaxis(a.reshape(bsz, nh, s // L, L, *a.shape[3:]), 2, 0)
    state, out = lax.scan(step, state, tuple(to_blocks(a) for a in seqs))
    out = jnp.moveaxis(out, 0, 2)
    bsz, nh, nc, l, d = out.shape
    return state, out.reshape(bsz, nh, nc * l, d)

def hybrid_mixer(hn, pos, C, n, m, R, w_in, b_gates, g_gn_mlstm, g_gn_ret, w_out):
    f32 = jnp.float32
    S = hn.shape[1]
    L = min(CHUNK, S)
    proj = jnp.einsum('bsd,de->bse', hn, w_in).astype(f32)
    sizes = [D_MLSTM] * 4 + [D_RET] * 4 + [H_M, H_M]
    offs = np.cumsum(sizes)[:-1].tolist()
    mq, mk, mv, mo, rq, rk, rv, rg, i_pre, f_pre = jnp.split(proj, offs, axis=-1)
    bg = b_gates.astype(f32)
    q = heads(mq, H_M)
    k = heads(mk, H_M) * (DH_M ** -0.5)
    v = heads(mv, H_M)
    ig = jnp.transpose(i_pre + bg[:H_M], (0, 2, 1))
    lf = jnp.transpose(jax.nn.log_sigmoid(f_pre + bg[H_M:]), (0, 2, 1))
    (C_new, n_new, m_new), h_m = chunked_scan(mlstm_chunk, (C, n, m), (q, k, v, ig, lf), L)
    y_m = jax.nn.sigmoid(mo) * head_group_norm(h_m, g_gn_mlstm)
    qr = rope(heads(rq, H_R), pos)
    kr = rope(heads(rk, H_R), pos) * (DH_R ** -0.5)
    vr = heads(rv, H_R)
    R_new, h_r = chunked_scan(retention_chunk, R, (qr, kr, vr), L)
    y_r = jax.nn.silu(rg) * head_group_norm(h_r, g_gn_ret)
    y = jnp.concatenate([y_m, y_r], axis=-1).astype(hn.dtype) @ w_out
    return y, (C_new, n_new, m_new, R_new)

def trunk_layer(x, pos, C, n, m, R, g_ffn1, w_ffn1_gate, w_ffn1_up, w_ffn1_down, g_mix, w_in, b_gates,
                g_gn_mlstm, g_gn_ret, w_out, g_ffn2, w_ffn2_gate, w_ffn2_up, w_ffn2_down):
    x = x + 0.5 * swiglu(rms_norm(x, g_ffn1), w_ffn1_gate, w_ffn1_up, w_ffn1_down)
    y, st = hybrid_mixer(rms_norm(x, g_mix), pos, C, n, m, R, w_in, b_gates, g_gn_mlstm, g_gn_ret, w_out)
    x = x + y
    x = x + 0.5 * swiglu(rms_norm(x, g_ffn2), w_ffn2_gate, w_ffn2_up, w_ffn2_down)
    return x, st

def setup_inputs(seed: int = 0) -> dict:
    key = jax.random.key(seed)
    ks = jax.random.split(key, 24)
    nrm = jax.random.normal
    gain = lambda k, d: 1.0 + 0.02 * nrm(k, (DEPTH, d), jnp.float32)
    b_gates = jnp.concatenate([
        0.1 * nrm(ks[10], (DEPTH, H_M), jnp.float32),
        jnp.linspace(3.0, 6.0, H_M, dtype=jnp.float32)[None, :] + 0.1 * nrm(ks[11], (DEPTH, H_M), jnp.float32)], axis=-1)
    return {
        "x_prompt": nrm(ks[0], (BATCH, SEQ, D_MODEL), jnp.float32),
        "x_sample": nrm(ks[1], (DEC_BATCH, DEC_SEQ, D_MODEL), jnp.float32),
        "state_mlstm_C": 0.1 * nrm(ks[2], (DEPTH, DEC_BATCH, H_M, DH_M, DH_M), jnp.float32),
        "state_mlstm_n": 0.1 * nrm(ks[3], (DEPTH, DEC_BATCH, H_M, DH_M), jnp.float32),
        "state_mlstm_m": 0.5 * nrm(ks[4], (DEPTH, DEC_BATCH, H_M), jnp.float32),
        "state_ret_R": 0.1 * nrm(ks[5], (DEPTH, DEC_BATCH, H_R, DH_R, DH_R), jnp.float32),
        "g_ffn1": gain(ks[6], D_MODEL),
        "w_ffn1_gate": nrm(ks[7], (DEPTH, D_MODEL, D_FF), jnp.float32) * D_MODEL ** -0.5,
        "w_ffn1_up": nrm(ks[8], (DEPTH, D_MODEL, D_FF), jnp.float32) * D_MODEL ** -0.5,
        "w_ffn1_down": nrm(ks[9], (DEPTH, D_FF, D_MODEL), jnp.float32) * D_FF ** -0.5,
        "g_mix": gain(ks[12], D_MODEL),
        "w_in": nrm(ks[13], (DEPTH, D_MODEL, D_IN), jnp.float32) * D_MODEL ** -0.5,
        "b_gates": b_gates,
        "g_gn_mlstm": gain(ks[14], D_MLSTM),
        "g_gn_ret": gain(ks[15], D_RET),
        "w_out": nrm(ks[16], (DEPTH, D_MIX, D_MODEL), jnp.float32) * D_MIX ** -0.5,
        "g_ffn2": gain(ks[17], D_MODEL),
        "w_ffn2_gate": nrm(ks[18], (DEPTH, D_MODEL, D_FF), jnp.float32) * D_MODEL ** -0.5,
        "w_ffn2_up": nrm(ks[19], (DEPTH, D_MODEL, D_FF), jnp.float32) * D_MODEL ** -0.5,
        "w_ffn2_down": nrm(ks[20], (DEPTH, D_FF, D_MODEL), jnp.float32) * D_FF ** -0.5,
        "g_final": 1.0 + 0.02 * nrm(ks[21], (D_MODEL,), jnp.float32),
    }

def reference(x_prompt, x_sample, state_mlstm_C, state_mlstm_n, state_mlstm_m, state_ret_R,
              g_ffn1, w_ffn1_gate, w_ffn1_up, w_ffn1_down, g_mix, w_in, b_gates, g_gn_mlstm, g_gn_ret,
              w_out, g_ffn2, w_ffn2_gate, w_ffn2_up, w_ffn2_down, g_final):
    f32 = jnp.float32
    Bp, Sp = x_prompt.shape[0], x_prompt.shape[1]
    pos_p = jnp.arange(Sp)
    pos_s = PAST_LEN + jnp.arange(x_sample.shape[1])
    hp, hs = x_prompt, x_sample
    new_p, new_s = [], []
    for l in range(DEPTH):
        w = (g_ffn1[l], w_ffn1_gate[l], w_ffn1_up[l], w_ffn1_down[l], g_mix[l], w_in[l], b_gates[l],
             g_gn_mlstm[l], g_gn_ret[l], w_out[l], g_ffn2[l], w_ffn2_gate[l], w_ffn2_up[l], w_ffn2_down[l])
        hp, sp = trunk_layer(hp, pos_p,
                             jnp.zeros((Bp, H_M, DH_M, DH_M), f32), jnp.zeros((Bp, H_M, DH_M), f32),
                             jnp.zeros((Bp, H_M), f32), jnp.zeros((Bp, H_R, DH_R, DH_R), f32), *w)
        hs, ss = trunk_layer(hs, pos_s,
                             state_mlstm_C[l].astype(f32), state_mlstm_n[l].astype(f32),
                             state_mlstm_m[l].astype(f32), state_ret_R[l].astype(f32), *w)
        new_p.append(sp)
        new_s.append(ss)
    y_prompt = rms_norm(hp, g_final)
    y_sample = rms_norm(hs, g_final)
    C_p = jnp.stack([s[0] for s in new_p])
    n_p = jnp.stack([s[1] for s in new_p])
    m_p = jnp.stack([s[2] for s in new_p])
    R_p = jnp.stack([s[3] for s in new_p])
    C_s = jnp.stack([s[0] for s in new_s])
    n_s = jnp.stack([s[1] for s in new_s])
    m_s = jnp.stack([s[2] for s in new_s])
    R_s = jnp.stack([s[3] for s in new_s])
    return (y_prompt, y_sample, C_p, n_p, m_p, R_p, C_s, n_s, m_s, R_s)


_drawn_inputs = setup_inputs


def setup_inputs(seed=0):
    import zlib

    import numpy as np

    out = dict(_drawn_inputs(seed))
    spreads = {}
    factors = {'g_ffn1': 3.336, 'g_gn_mlstm': 8.0, 'g_gn_ret': 7.545, 'g_ffn2': 8.0, 'g_final': 2.743}
    for name, (base, spread) in spreads.items():
        noise = np.random.default_rng([zlib.crc32(name.encode()), seed]).standard_normal(out[name].shape)
        drawn = base * np.exp(spread * noise) if base else spread * noise
        out[name] = __import__('jax').numpy.asarray(drawn.astype(out[name].dtype))
    for name, factor in factors.items():
        out[name] = (out[name] * factor).astype(out[name].dtype)
    return out
```

```python
from contextlib import ExitStack

import numpy as np

import concourse.bass as bass
from concourse import mybir

ALU = mybir.AluOpType
ACT = mybir.ActivationFunctionType
F32 = mybir.dt.float32
F32R = mybir.dt.float32r

P = 128
H = 4
EPS = 1e-6
GN_EPS = 1e-5
PAST_LEN = 1024
ROPE_BASE = 10000.0

LOG_GAMMA = np.log(1.0 - 2.0 ** (-5.0 - np.arange(H))).astype(np.float32)


def shape_tables(tp, ts):
    t = tp + ts
    half = P // 2
    inv = (np.float32(ROPE_BASE) ** (-np.arange(half, dtype=np.float32) / half)).astype(np.float32)
    pos = np.concatenate([np.arange(tp), PAST_LEN + np.arange(ts)]).astype(np.float32)
    ang = inv[:, None] * pos[None, :]
    cos = np.cos(ang).astype(np.float32)
    sin = np.sin(ang).astype(np.float32)
    idx = np.arange(P, dtype=np.float32)
    diff = idx[None, :] - idx[:, None]
    scale = np.float32(P ** -0.5)
    decay = [np.where(diff >= 0, np.exp(lg * np.maximum(diff, 0)), 0).astype(np.float32) * scale for lg in LOG_GAMMA]
    cross = [np.broadcast_to(np.exp(lg * (idx + 1)), (P, P)) for lg in LOG_GAMMA]
    tail = np.stack([np.exp(lg * (P - 1 - idx)) * scale for lg in LOG_GAMMA], 1)
    tail_s = np.stack([np.exp(lg * np.maximum(ts - 1 - idx, 0)) * scale for lg in LOG_GAMMA], 1)
    cols = [np.concatenate([cos, cos]), np.concatenate([sin, -sin]), *decay, *cross, tail, tail_s]
    table = np.ascontiguousarray(np.concatenate(cols, axis=1).astype(np.float32))
    assert table.shape == (P, 2 * t + 8 * P + 8)
    return table


def hybrid_trunk_step(nc, x_prompt, x_sample, state_mlstm_C, state_mlstm_n, state_mlstm_m, state_ret_R,
                      g_ffn1, w_ffn1_gate, w_ffn1_up, w_ffn1_down, g_mix, w_in, b_gates, g_gn_mlstm, g_gn_ret,
                      w_out, g_ffn2, w_ffn2_gate, w_ffn2_up, w_ffn2_down, g_final, tables,
                      y_prompt, y_sample, C_prompt, n_prompt, m_prompt, R_prompt, C_sample, n_sample, m_sample,
                      R_sample):
    TP, D = x_prompt.shape[1], x_prompt.shape[2]
    TS = x_sample.shape[1]
    T = TP + TS
    TH = T // 2
    DT = D // P
    F = w_ffn1_gate.shape[2]
    FT = F // P
    NC = TP // P
    CH = [slice(c * P, (c + 1) * P) for c in range(NC)] + [slice(TP, T)]
    V1 = P + 1
    assert D == 8 * P and T % 2 == 0 and TH <= 512 and TP == 512 and TS == 32

    DOWN_K = [(0, 6), (6, 12), (12, 17), (17, FT)]
    U_F1 = 0
    U_D1 = U_F1 + 2 * FT
    U_GATE = U_D1 + 4 * DT
    U_IN = U_GATE + 1
    U_OUT = U_IN + 8 * H
    U_F2 = U_OUT + DT
    U_D2 = U_F2 + 2 * FT
    U_END = U_D2 + 4 * DT
    T_X = 0
    T_F1 = T_X + DT
    T_D1 = T_F1 + 2 * FT
    T_GATE = T_D1 + DT
    T_IN = T_GATE + 1
    T_OUT = T_IN + 8 * H
    T_F2 = T_OUT + DT
    T_D2 = T_F2 + 2 * FT

    def k_tiles(s):
        for base in (U_D1, U_D2):
            if base <= s < base + 4 * DT:
                a, b = DOWN_K[(s - base) % 4]
                return b - a
        return DT

    def groups(eng, base, count, step, body):
        n = count // step
        body(0, base, 0)
        with eng.Fori(0, n - 2) as i:
            body(i, base + step, 1)
        body(0, base + step * (n - 1), n - 1)

    with ExitStack() as ctx:
        at = {"next": -(-nc.sbuf_base // 32) * 32}

        def sb(name, shape, dt=F32):
            handle = nc.alloc_sbuf_tensor_at(name, shape, dt, offset=at["next"])
            at["next"] += -(-int(np.prod(shape[1:])) * 4 // 32) * 32
            return handle

        def sem(name):
            return ctx.enter_context(nc.semaphore(name))


        xT = sb("xT", [P, DT, T])
        w_raw = sb("w_raw", [P, 2, DT, P])
        w_hi = sb("w_hi", [P, 4, DT, P], F32R)
        w_lo = sb("w_lo", [P, 4, DT, P], F32R)
        rstd = sb("rstd", [P, T])
        sq = sb("sq", [P, T])
        sq_sum = sb("sq_sum", [P, T])
        ident = sb("ident", [P, P])
        ones = sb("ones", [P, P])
        gains = sb("gains", [P, 5 * DT])
        eps = sb("eps", [P, 1])
        w_gates = sb("w_gates", [P, DT, 2 * H])
        row_small = sb("row_small", [H, 16])
        G_FFN1, G_MIX, G_FFN2, G_FINAL, G_GN = (DT * n for n in range(5))

        xg_region = at["next"]
        xg_hi = sb("xg_hi", [P, DT, T], F32R)
        xg_lo = sb("xg_lo", [P, DT, T], F32R)
        xg_end = at["next"]
        at["next"] = xg_region
        y_tok = sb("y_tok", [P, NC + 1, D])
        x_gain = sb("x_gain", [P, 2, T])
        rms_tok = sb("rms_tok", [P, 2, NC + 1])
        assert at["next"] <= xg_end

        at["next"] = stage_region = xg_end
        x_tok = sb("x_tok", [P, NC + 1, D])
        gain_rows = sb("gain_rows", [5 * DT, P])

        at["next"] = stage_region
        h_hi = sb("h_hi", [P, FT, T], F32R)
        h_lo = sb("h_lo", [P, FT, T], F32R)
        gate_n = sb("gate_n", [P, T])
        gate_s = sb("gate_s", [P, T])
        gate_r = sb("gate_r", [P, T])
        h_f = sb("h_f", [P, T])
        ffn_end = at["next"]

        at["next"] = stage_region
        y_hi_m = sb("y_hi_m", [P, H, T], F32R)
        y_lo_m = sb("y_lo_m", [P, H, T], F32R)
        y_ret_region = at["next"]
        y_hi_r = sb("y_hi_r", [P, H, T], F32R)
        y_lo_r = sb("y_lo_r", [P, H, T], F32R)
        y_ret_end = at["next"]
        at["next"] = y_ret_region
        rows = sb("rows", [H, 5, T])
        row_cols = sb("row_cols", [64, T])
        sel = sb("sel", [H, H, P])
        assert at["next"] <= y_ret_end
        at["next"] = y_ret_end
        proj = sb("proj", [P, 2, 4, T])
        table = sb("table", [P, tables.shape[1]])
        state_in = sb("state_in", [P, 2 * H, V1])
        state_p = sb("state_p", [P, 2 * H, V1])
        state_s = sb("state_s", [P, 2 * H, V1])
        chain = sb("chain", [P, NC - 1, V1])
        weights_arg = sb("weights_arg", [P, T])
        weights = sb("weights", [P, T])
        past = sb("past", [P, T])
        q_past = sb("q_past", [P, T])
        scores = sb("scores", [P, T])
        k_tail = sb("k_tail", [P, NC + 1, P])
        v_tok = sb("v_tok", [P, NC + 1, V1])
        o_tok = sb("o_tok", [P, NC + 1, V1])
        gate_act = sb("gate_act", [P, T])
        y_f = sb("y_f", [P, T])
        rot = sb("rot", [P, 2, T])
        mask = sb("mask", [P, P])
        key_col = sb("key_col", [P, NC + 1, H])
        neg_m_exp = sb("neg_m_exp", [P, NC + 1, H])
        m_prev_all = sb("m_prev_all", [P, H, NC + 1])
        stats = sb("stats", [P, NC + 1, 6])
        mean_var = sb("mean_var", [P, NC + 1, 2])
        small = sb("small", [P, 8, NC + 1])
        mixer_end = at["next"]
        at["next"] = max(ffn_end, mixer_end)
        assert at["next"] <= nc.sbuf_usable_end, (at["next"], nc.sbuf_usable_end, ffn_end, mixer_end)

        I_ROW, F_ROW, E_ROW, LF_ROW, M_ROW = range(5)
        B_ROW, BM_ROW = F_ROW, E_ROW
        M_PREV, M_OUT = 4, 9
        ACT_CHUNKS = (NC - 1, NC)
        COS, SIN, DECAY, CROSS = 0, T, 2 * T, 2 * T + H * P
        TAIL, TAIL_S = CROSS + H * P, CROSS + H * P + H

        dense = [ctx.enter_context(nc.psum_tensor(f"dense{n}", [P, 2, 512], F32)) for n in range(2)]
        X = ctx.enter_context(nc.psum_tensor("core_banks", [P, 4, 512], F32))

        def y_hi(kt):
            return (y_hi_m if kt < H else y_hi_r)[:, kt % H, :]

        def y_lo(kt):
            return (y_lo_m if kt < H else y_lo_r)[:, kt % H, :]

        def halves(tile):
            return tile[:, :, 0:TH]

        def split_cols(ap):
            return ap.rearrange("p (a b) -> p a b", a=2)

        x_loaded = sem("x_loaded")
        gains_loaded = sem("gains_loaded")
        consts_ready = sem("consts_ready")
        gains_ready = sem("gains_ready")
        gains_moved = sem("gains_moved")
        w_loaded = [sem("w_loaded0"), sem("w_loaded1")]
        gates_loaded = sem("gates_loaded")
        gate_slots_zeroed = sem("gate_slots_zeroed")
        w_hi_ready = sem("w_hi_ready")
        w_lo_ready = sem("w_lo_ready")
        unit_done = sem("unit_done")
        x_moved = sem("x_moved")
        evicted = sem("evicted")
        sq_ready = sem("sq_ready")
        sq_added = sem("sq_added")
        xg_hi_ready = sem("xg_hi_ready")
        xg_lo_ready = sem("xg_lo_ready")
        norm_sums = sem("norm_sums")
        norm_root = sem("norm_root")
        rstd_ready = sem("rstd_ready")
        silu_ready = sem("silu_ready")
        silu_scaled = sem("silu_scaled")
        h_hi_ready = sem("h_hi_ready")
        h_lo_ready = sem("h_lo_ready")
        table_loaded = sem("table_loaded")
        mixer_consts = sem("mixer_consts")
        state_loaded = sem("state_loaded")
        gates_biased = sem("gates_biased")
        gates_ln = sem("gates_ln")
        gate_rows_ready = sem("gate_rows_ready")
        gate_cols_moved = sem("gate_cols_moved")
        gate_cols_ready = sem("gate_cols_ready")
        tables_scaled = sem("tables_scaled")
        rotated = sem("rotated")
        rot_terms = sem("rot_terms")
        rows_spread = sem("rows_spread")
        arg_ready = sem("arg_ready")
        weights_ready = sem("weights_ready")
        past_ready = sem("past_ready")
        q_past_ready = sem("q_past_ready")
        scores_done = sem("scores_done")
        scores_weighted = sem("scores_weighted")
        v_ready = sem("v_ready")
        gate_act_ready = sem("gate_act_ready")
        updates_done = sem("updates_done")
        states_ready = sem("states_ready")
        mixed_done = sem("mixed_done")
        o_ready = sem("o_ready")
        var_ready = sem("var_ready")
        root_ready = sem("root_ready")
        shift_ready = sem("shift_ready")
        normed = sem("normed")
        normed_act = sem("normed_act")
        turned = sem("turned")
        y_ready = sem("y_ready")
        y_hi_ready = sem("y_hi_ready")
        y_lo_ready = sem("y_lo_ready")
        x_gained = sem("x_gained")
        out_turned = sem("out_turned")
        out_taken = sem("out_taken")
        final_sums = sem("final_sums")
        final_root = sem("final_root")
        final_rstd = sem("final_rstd")
        y_done = [sem(f"y_done{c}") for c in range(NC + 1)]
        stored = sem("stored")
        act_step = sem("act_step")
        dve_step = sem("dve_step")
        pool_step = sem("pool_step")

        def chained(eng, s):
            count = [0]

            def link(ins):
                count[0] += 1
                ins.then_inc(s, 1)
                eng.wait_ge(s, count[0])

            return link

        def w_rows(w):
            return w[0].rearrange("(k p) n -> p k n", p=P)

        ffns = [(U_F1, T_F1, U_D1, T_D1, w_ffn1_gate, w_ffn1_up, w_ffn1_down),
                (U_F2, T_F2, U_D2, T_D2, w_ffn2_gate, w_ffn2_up, w_ffn2_down)]
        block = ctx.enter_context(nc.Block())

        @block.sync
        def _(sp):
            sp.dma_start(x_tok[:, 0:1, :], x_prompt[0, 0:P, :].rearrange("(c p) d -> p c d", p=P)).then_inc(x_loaded, 16)
            for n, g in enumerate((g_ffn1, g_mix, g_ffn2)):
                sp.dma_start(gain_rows[n * DT:(n + 1) * DT, :], g[0].rearrange("(k p) -> k p", p=P)).then_inc(gains_loaded, 16)
            sp.dma_start(gain_rows[G_FINAL:G_FINAL + DT, :], g_final.rearrange("(k p) -> k p", p=P)).then_inc(gains_loaded, 16)
            sp.dma_start(gain_rows[G_GN:G_GN + H, :], g_gn_mlstm[0].rearrange("(k p) -> k p", p=P)).then_inc(gains_loaded, 16)
            sp.dma_start(gain_rows[G_GN + H:G_GN + 2 * H, :], g_gn_ret[0].rearrange("(k p) -> k p", p=P)).then_inc(gains_loaded, 16)
            sp.dma_start(x_tok[:, 1:NC, :], x_prompt[0, P:TP, :].rearrange("(c p) d -> p c d", p=P)).then_inc(x_loaded, 16)
            sp.dma_start(x_tok[0:TS, NC, :], x_sample[0, :, :]).then_inc(x_loaded, 16)

            sp.dma_start(row_small[:, 0:1], b_gates[0, 0:H].rearrange("(h a) -> h a", a=1)).then_inc(gates_loaded, 16)
            sp.dma_start(row_small[:, 1:2], b_gates[0, H:2 * H].rearrange("(h a) -> h a", a=1)).then_inc(gates_loaded, 16)
            sp.dma_start(row_small[:, 2:3], state_mlstm_m[0, 0].rearrange("(h a) -> h a", a=1)).then_inc(gates_loaded, 16)

            def load(i, s, step, source, nk):
                if s >= 2:
                    sp.wait_ge(w_lo_ready, s - 1 + step * i)
                sp.dma_start(w_raw[:, s % 2, 0:nk, :], source).then_inc(w_loaded[s % 2], 16)

            def ffn(u_base, d_base, w_gate, w_up, w_down):
                gate_v, up_v, down_v = w_rows(w_gate), w_rows(w_up), w_rows(w_down)
                if u_base == 0:
                    for u in range(4):
                        load(0, u, 0, (gate_v, up_v)[u % 2][:, :, (u // 2) * P:(u // 2 + 1) * P], DT)
                    sp.dma_start(w_gates[:, :, :], w_rows(w_in)[:, :, 8 * H * P:8 * H * P + 2 * H]).then_inc(gates_loaded, 16)
                with sp.Fori(0 if u_base else 1, FT // 2) as i:
                    for u in range(4):
                        w = (gate_v, up_v)[u % 2]
                        col = i * (2 * P) + (u // 2) * P
                        sp.wait_ge(w_lo_ready, u_base + u - 1 + 4 * i)
                        sp.dma_start(w_raw[:, (u_base + u) % 2, :, :], w[:, :, bass.ds(col, P)])\
                          .then_inc(w_loaded[(u_base + u) % 2], 16)
                with sp.Fori(0, DT) as i:
                    for u, (a, b) in enumerate(DOWN_K):
                        load(i, d_base + u, 4, down_v[:, a:b, bass.ds(i * P, P)], b - a)

            ffn(U_F1, U_D1, w_ffn1_gate, w_ffn1_up, w_ffn1_down)

            in_v = w_rows(w_in)
            for h in range(2 * H):
                for u in range(4):
                    col = (h // H) * 4 * H * P + u * H * P + (h % H) * P
                    load(0, U_IN + 4 * h + u, 0, in_v[:, :, col:col + P], DT)
                if h == 0:
                    sp.wait_ge(unit_done, U_GATE)
                    sp.dma_start(table[:, :], tables[:, :]).then_inc(table_loaded, 16)
                    sp.dma_start(state_in[:, 0:H, 0:P], state_mlstm_C[0, 0].rearrange("h d e -> d h e")).then_inc(state_loaded, 16)
                    sp.dma_start(state_in[:, H:2 * H, 0:P], state_ret_R[0, 0].rearrange("h d e -> d h e")).then_inc(state_loaded, 16)
                    for hh in range(H):
                        sp.dma_start(state_in[:, hh, P:V1], state_mlstm_n[0, 0, hh].rearrange("(d a) -> d a", a=1)).then_inc(state_loaded, 16)
            out_v = w_rows(w_out)
            for j in range(DT):
                load(0, U_OUT + j, 0, out_v[:, :, j * P:(j + 1) * P], DT)
            sp.wait_ge(states_ready, 2 * H)
            stores = 0
            for state, C_out, n_out, R_out in ((state_p, C_prompt, n_prompt, R_prompt), (state_s, C_sample, n_sample, R_sample)):
                sp.dma_start(C_out[0, 0].rearrange("h d e -> d h e"), state[:, 0:H, 0:P]).then_inc(stored, 16)
                sp.dma_start(R_out[0, 0].rearrange("h d e -> d h e"), state[:, H:2 * H, 0:P]).then_inc(stored, 16)
                for hh in range(H):
                    sp.dma_start(n_out[0, 0, hh].rearrange("(d a) -> d a", a=1), state[:, hh, P:V1]).then_inc(stored, 16)
                stores += 2 + H
            for out_m, t in ((m_prompt, M_OUT), (m_sample, M_OUT + 1)):
                sp.dma_start(out_m[0, 0].rearrange("(h a) -> h a", a=1), row_small[:, t:t + 1]).then_inc(stored, 16)
                stores += 1
            sp.wait_ge(stored, 16 * stores)

            ffn(U_F2, U_D2, w_ffn2_gate, w_ffn2_up, w_ffn2_down)

            for c in range(NC + 1):
                sp.wait_ge(y_done[c], 1)
                if c < NC:
                    sp.dma_start(y_prompt[0, CH[c], :], y_tok[:, c, :]).then_inc(stored, 16)
                else:
                    sp.dma_start(y_sample[0, :, :], y_tok[0:TS, c, :]).then_inc(stored, 16)
            sp.wait_ge(stored, 16 * (stores + NC + 1))

        @block.tensor
        def _(pe):
            def product(s, out, x_hi, x_lo, kts, start, stop, i=0, step=0, slot_k0=0, ready=None):
                for n, kt in enumerate(kts):
                    if ready is not None:
                        ready(kt)
                    k = kt - slot_k0
                    passes = [(w_hi, x_hi), (w_hi, x_lo), (w_lo, x_hi)]
                    for m, (w, x) in enumerate(passes):
                        for half in range(2):
                            last = nc.tensor.matmul(
                                out[:, half, 0:TH], w[:, s % 4, k, :], x(kt)[:, half * TH:(half + 1) * TH],
                                start=start and n == 0 and m == 0, stop=stop and n == len(kts) - 1 and m == 2)
                return last

            xg = (lambda kt: xg_hi[:, kt, :]), (lambda kt: xg_lo[:, kt, :])
            h_halves = (lambda kt: h_hi[:, kt, :]), (lambda kt: h_lo[:, kt, :])

            def tile_free(t, i=0, step=0):
                pe.wait_ge(evicted, t - 1 + step * i)

            def norm_sums_of(n):
                pe.wait_ge(sq_added, DT * (n + 1))
                for half in range(2):
                    last = nc.tensor.matmul(X[:, half, 0:TH], ones[:, :], sq_sum[:, half * TH:(half + 1) * TH], start=True, stop=True)
                last.then_inc(norm_sums, 1)

            def xg_ready(n):
                return lambda kt: pe.wait_ge(xg_lo_ready, DT * n + kt + 1)

            def ffn(n, u_base, t_base, d_base, td_base, norm):
                def gate_up(i, s, g):
                    for u in range(4):
                        pe.wait_ge(w_lo_ready, s + u + 1 + 4 * i)
                        t = t_base + s - u_base + u
                        tile_free(t, i, 4)
                        first = g == 0 and u == 0
                        product(s + u, dense[t % 2], *xg, range(DT), True, True,
                                ready=xg_ready(norm) if first else None).then_inc(unit_done, 1)
                        if first:
                            if n:
                                pe.wait_ge(y_ready, 2 * H)
                            norm_sums_of(norm)

                groups(pe, u_base, 2 * FT, 4, gate_up)

                def down(i, s, g):
                    for v in range(2):
                        t = td_base + 2 * g + v
                        for u, (a, b) in enumerate(DOWN_K):
                            unit = s + 4 * v + u
                            pe.wait_ge(w_lo_ready, unit + 1 + 8 * i)
                            if u == 0:
                                tile_free(t, i, 2)
                            if g == 0 and v == 0:
                                pe.wait_ge(h_lo_ready, FT * n + b)
                            product(unit, dense[t % 2], *h_halves, range(a, b), u == 0, u == 3, slot_k0=a).then_inc(unit_done, 1)
                            if n and u == 0 and not (g == 0 and v == 0):
                                turn_out(i, 2 * g + v - 1)

                groups(pe, d_base, 4 * DT, 8, down)

            def turn_out(i, j):
                pe.wait_ge(x_gained, j + 1 + 2 * i)
                b = 2 * (j % 2)
                if j >= 2:
                    pe.wait_ge(out_taken, j - 1 + 2 * i)
                for c in range(NC):
                    nc.tensor.transpose(X[:, b, CH[c]], x_gain[:, j % 2, CH[c]], ident[:, :])
                nc.tensor.transpose(X[0:TS, b + 1, 0:P], x_gain[:, j % 2, TP:T], ident[:, :]).then_inc(out_turned, 1)

            pe.wait_ge(consts_ready, 3)
            pe.wait_ge(gains_loaded, 16 * 6)
            nc.tensor.transpose(X[:, 0, 0:5 * DT], gain_rows[:, :], ident[0:5 * DT, 0:5 * DT]).then_inc(gains_moved, 1)
            pe.wait_ge(x_loaded, 16 * 3)
            for j in range(DT):
                if j >= 2:
                    tile_free(T_X + j)
                flat = dense[j % 2][:, :, :].rearrange("p a b -> p (a b)")
                for c in range(NC):
                    nc.tensor.transpose(flat[:, CH[c]], x_tok[:, c, j * P:(j + 1) * P], ident[:, :])
                nc.tensor.transpose(flat[:, TP:T], x_tok[0:TS, NC, j * P:(j + 1) * P], ident[0:TS, 0:TS]).then_inc(x_moved, 1)

            pe.wait_ge(gains_ready, 1)
            ffn(0, U_F1, T_F1, U_D1, T_D1, 0)

            def p(h, what, cols):
                return proj[:, h % 2, what, cols]

            def step_scores(h):
                if h < H:
                    pe.wait_ge(evicted, T_IN + 4 * h + 3)
                    pe.wait_ge(past_ready, h + 1)
                else:
                    pe.wait_ge(rotated, 2 * (h - H) + 2)
                    pe.wait_ge(evicted, T_IN + 4 * h + 3)
                    pe.wait_ge(o_ready, h)
                if h:
                    pe.wait_ge(y_ready, h)
                for c in range(NC):
                    nc.tensor.transpose(X[:, 0, CH[c]], p(h, 1, CH[c]), ident[:, :])
                for c in range(NC):
                    nc.tensor.transpose(X[:, 1, CH[c]], p(h, 2, CH[c]), ident[:, :])
                nc.tensor.transpose(X[0:TS, 2, 0:P], p(h, 1, CH[NC]), ident[:, :])
                nc.tensor.transpose(X[0:TS, 2, P:2 * P], p(h, 2, CH[NC]), ident[:, :])
                for c in range(NC):
                    nc.tensor.matmul(X[:, 3, CH[c]], p(h, 1, CH[c]), p(h, 0, CH[c]), start=True, stop=True)
                nc.tensor.matmul(X[0:TS, 2, 2 * P:2 * P + TS], p(h, 1, CH[NC]), p(h, 0, CH[NC]),
                                 start=True, stop=True).then_inc(scores_done, 1)

            def step_updates(h):
                pe.wait_ge(scores_weighted, h + 1)
                pe.wait_ge(v_ready, h + 1)
                for c in range(NC + 1):
                    n = P if c < NC else TS
                    b, o = (0, c) if c < 3 else (1, c - 3)
                    last = nc.tensor.matmul(X[:, b, o * V1:(o + 1) * V1], k_tail[0:n, c, :], v_tok[0:n, c, :],
                                            start=True, stop=True)
                last.then_inc(updates_done, 1)

            def step_mix(h):
                pe.wait_ge(states_ready, h + 1)
                pe.wait_ge(q_past_ready, h + 1)
                if h == 0:
                    pe.wait_ge(state_loaded, 16 * (2 + H))
                for c in range(NC + 1):
                    n = P if c < NC else TS
                    b, o = (2, c) if c < 3 else (3, c - 3)
                    out = X[0:n, b, o * V1:(o + 1) * V1]
                    last = nc.tensor.matmul(out, scores[0:n, CH[c]], v_tok[0:n, c, :], start=True, stop=c == 0)
                    if c:
                        state = chain[:, c - 1, :] if c < NC else state_in[:, h, :]
                        last = nc.tensor.matmul(out, q_past[:, CH[c]], state, start=False, stop=True)
                last.then_inc(mixed_done, 1)

            def step_turn(h):
                pe.wait_ge(normed, h + 1)
                pe.wait_ge(normed_act, h + 1)
                flat = X[:, 0:2, :].rearrange("p a b -> p (a b)")
                for c in range(NC):
                    nc.tensor.transpose(flat[:, CH[c]], o_tok[:, c, 0:P], ident[:, :])
                nc.tensor.transpose(flat[:, TP:T], o_tok[0:TS, NC, 0:P], ident[0:TS, 0:TS]).then_inc(turned, 1)

            def step_rows(h):
                if h == 0:
                    pe.wait_ge(gate_cols_ready, 1)
                else:
                    pe.wait_ge(o_ready, h)
                nc.tensor.matmul(X[:, 2, :], sel[:, h, :], rows[:, BM_ROW, 0:TP], start=True, stop=True)
                nc.tensor.matmul(X[:, 3, 0:TS], sel[:, h, :], rows[:, BM_ROW, TP:T], start=True, stop=True).then_inc(rows_spread, 1)

            def gate_columns():
                pe.wait_ge(gate_rows_ready, 1)
                for c in range(NC):
                    nc.tensor.transpose(X[:, 2, c * 64:(c + 1) * 64], row_cols[:, CH[c]], ident[0:64, 0:64])
                nc.tensor.transpose(X[0:TS, 2, NC * 64:(NC + 1) * 64], row_cols[:, TP:T], ident[0:64, 0:64])
                for h in range(H):
                    last = nc.tensor.matmul(X[:, 3, h * (NC + 1):(h + 1) * (NC + 1)], sel[:, h, :],
                                            row_small[:, M_PREV:M_PREV + NC + 1], start=True, stop=True)
                last.then_inc(gate_cols_moved, 1)

            pe.wait_ge(w_lo_ready, U_GATE + 1)
            tile_free(T_GATE)
            product(U_GATE, dense[T_GATE % 2], *xg, range(DT), True, True, ready=xg_ready(1)).then_inc(unit_done, 1)
            norm_sums_of(1)
            for h in range(2 * H):
                for u in range(4):
                    s, t = U_IN + 4 * h + u, T_IN + 4 * h + u
                    pe.wait_ge(w_lo_ready, s + 1)
                    tile_free(t)
                    product(s, dense[t % 2], *xg, range(DT), True, True).then_inc(unit_done, 1)
                    if h == 0 and u == 1:
                        gate_columns()
                    if u == 2 and h < H:
                        step_rows(h)
                    if u == 3:
                        step_scores(h)
                    elif h:
                        (step_updates, step_mix, step_turn)[u](h - 1)
            for j, part, step in ((0, range(0, 4), step_updates), (0, range(4, DT - 1), step_mix), (1, range(0, DT - 1), step_turn)):
                if part[0] == 0:
                    pe.wait_ge(w_lo_ready, U_OUT + j + 1)
                    tile_free(T_OUT + j)
                if j == 0:
                    pe.wait_ge(y_lo_ready, part[-1] + 1)
                product(U_OUT + j, dense[(T_OUT + j) % 2], y_hi, y_lo, part, part[0] == 0, False)
                step(2 * H - 1)
            pe.wait_ge(y_lo_ready, 2 * H)
            for j in range(2):
                product(U_OUT + j, dense[(T_OUT + j) % 2], y_hi, y_lo, [DT - 1], False, True).then_inc(unit_done, 1)
            for j in range(2, DT):
                pe.wait_ge(w_lo_ready, U_OUT + j + 1)
                tile_free(T_OUT + j)
                product(U_OUT + j, dense[(T_OUT + j) % 2], y_hi, y_lo, range(DT), True, True).then_inc(unit_done, 1)

            ffn(1, U_F2, T_F2, U_D2, T_D2, 2)
            turn_out(0, DT - 1)
            pe.wait_ge(out_taken, DT - 1)
            pe.wait_ge(sq_added, DT * 4)
            for c in range(NC + 1):
                n = P if c < NC else TS
                last = nc.tensor.matmul(X[0:n, 0, c:c + 1], sq_sum[:, CH[c]], ones[:, 0:1], start=True, stop=True)
            last.then_inc(final_sums, 1)

        @block.scalar
        def _(act):
            link = chained(act, act_step)


            def split_hi(i, s, step):
                if s >= U_END:
                    return
                if s == U_GATE:
                    act.wait_ge(gates_loaded, 16 * 4)
                    act.wait_ge(gate_slots_zeroed, 2)
                    for n in range(2):
                        last = nc.scalar.activation(w_hi[:, s % 4, :, 32 * n:32 * n + H], w_gates[:, :, H * n:H * (n + 1)], ACT.Copy)
                    last.then_inc(w_hi_ready, 1)
                    return
                loads = len([m for m in range(s % 2, s + 1, 2) if m != U_GATE])
                act.wait_ge(w_loaded[s % 2], 16 * loads + 8 * step * i)
                source = w_raw[:, s % 2, 0:k_tiles(s), :]
                if s >= 4:
                    act.wait_ge(unit_done, s - 3 + step * i)
                nc.scalar.activation(w_hi[:, s % 4, 0:k_tiles(s), :], source, ACT.Copy).then_inc(w_hi_ready, 1)

            def square(j, norm):
                if norm or j:
                    act.wait_ge(sq_added, DT * norm + j)
                nc.scalar.activation(sq[:, :], xT[:, j, :], ACT.Square).then_inc(sq_ready, 1)

            def normed_hi(i, j, t, g, step):
                act.wait_ge(evicted, t + 1 + step * i)
                act.wait_ge(gains_ready, 1)
                nc.scalar.activation(xg_hi[:, j + step * i, :], xT[:, j + step * i, :], ACT.Copy,
                                     scale=gains[:, bass.ds(g + j + step * i, 1)]).then_inc(xg_hi_ready, 1)

            def root(n):
                act.wait_ge(norm_sums, n + 1)
                nc.scalar.activation(rstd[:, :].rearrange("p (a b) -> p a b", a=2), X[:, 0:2, 0:TH], ACT.Sqrt, scale=1.0 / D,
                                     bias=eps[:, :]).then_inc(norm_root, 1)

            def ffn(n, u_base, t_base, d_base, td_base, norm):
                def gate_up(i, s, g):
                    for u in range(4):
                        split_hi(i, s + u + 2, 4)
                        t = t_base + s - u_base + u
                        j = 2 * g + u // 2
                        if g == 0 and u == 0:
                            root(norm)
                        act.wait_ge(evicted, t + 1 + 4 * i)
                        if u % 2 == 0:
                            if n or j:
                                act.wait_ge(silu_scaled, FT * n + j + 2 * i)
                            nc.scalar.activation(gate_s[:, :], gate_n[:, :], ACT.Silu).then_inc(silu_ready, 1)
                        else:
                            act.wait_ge(gains_ready, 1)
                            nc.scalar.activation(h_hi[:, j + 2 * i, :], h_f[:, :], ACT.Copy).then_inc(h_hi_ready, 1)

                groups(act, u_base, 2 * FT, 4, gate_up)

                def down(i, s, g):
                    for v in range(2):
                        for u in range(4):
                            split_hi(i, s + 4 * v + u + 2, 8)
                        j = 2 * g + v
                        if n == 0:
                            normed_hi(i, j, td_base + j, G_MIX, 2)
                        else:
                            act.wait_ge(evicted, td_base + j + 1 + 2 * i)
                            if j >= 2:
                                act.wait_ge(out_turned, j - 1 + 2 * i)
                            act.wait_ge(gains_ready, 1)
                            nc.scalar.activation(x_gain[:, j % 2, :], xT[:, j + 2 * i, :], ACT.Copy,
                                                 scale=gains[:, bass.ds(G_FINAL + j + 2 * i, 1)]).then_inc(x_gained, 1)

                groups(act, d_base, 4 * DT, 8, down)

            act.wait_ge(consts_ready, 3)
            act.wait_ge(gains_moved, 1)
            nc.scalar.activation(gains[:, :], X[:, 0, 0:5 * DT], ACT.Copy).then_inc(gains_ready, 1)
            act.wait_ge(gains_ready, 1)
            for j in range(DT):
                normed_hi(0, j, T_X + j, G_FFN1, 0)
                square(j, 0)
                if j in (2, 5):
                    split_hi(0, j // 3, 0)

            ffn(0, U_F1, T_F1, U_D1, T_D1, 0)

            def step_values(h):
                act.wait_ge(scores_done, h + 1)
                if h:
                    act.wait_ge(mixed_done, h)
                if h == 0:
                    act.wait_ge(mixer_consts, 1)
                if h == H:
                    act.wait_ge(table_loaded, 16)
                if h >= H:
                    nc.scalar.activation(k_tail[:, 0:NC, :], X[:, 0, :].rearrange("p (c d) -> p c d", c=NC), ACT.Copy,
                                         scale=table[:, TAIL + h - H:TAIL + h - H + 1])
                nc.scalar.activation(v_tok[:, 0:NC, 0:P], X[:, 1, :].rearrange("p (c d) -> p c d", c=NC), ACT.Copy)\
                    .then_inc(v_ready, 1)

            def step_gate(h):
                act.wait_ge(evicted, T_IN + 4 * h + 4)
                if h:
                    act.wait_ge(y_ready, h)
                nc.scalar.activation(gate_act[:, :], proj[:, h % 2, 3, :], ACT.Sigmoid if h < H else ACT.Silu)\
                    .then_inc(gate_act_ready, 1)

            def step_o(h):
                act.wait_ge(mixed_done, h + 1)
                if h:
                    act.wait_ge(turned, h)
                nc.scalar.activation(o_tok[:, 0:3, :], X[:, 2, 0:3 * V1].rearrange("p (c d) -> p c d", c=3), ACT.Copy)
                nc.scalar.activation(o_tok[:, 3, :], X[:, 3, 0:V1], ACT.Copy)
                nc.scalar.activation(o_tok[0:TS, NC, :], X[0:TS, 3, V1:2 * V1], ACT.Copy).then_inc(o_ready, 1)
                act.wait_ge(shift_ready, h + 1)
                for c in ACT_CHUNKS:
                    n = P if c < NC else TS
                    last = nc.scalar.activation(o_tok[0:n, c, 0:P], o_tok[0:n, c, 0:P], ACT.Identity,
                                                scale=small[0:n, 4, c:c + 1], bias=small[0:n, 5, c:c + 1])
                last.then_inc(normed_act, 1)

            def step_y(h):
                act.wait_ge(y_ready, h + 1)
                nc.scalar.activation(y_hi(h), y_f[:, :], ACT.Copy).then_inc(y_hi_ready, 1)

            def step_weights(h):
                act.wait_ge(arg_ready, h + 1)
                if h:
                    act.wait_ge(scores_weighted, h)
                for c in range(NC + 1):
                    n = P if c < NC else TS
                    last = nc.scalar.activation(weights[0:n, CH[c]], weights_arg[0:n, CH[c]], ACT.Exp,
                                                bias=key_col[0:n, c, h:h + 1])
                last.then_inc(weights_ready, 1)
                if h:
                    act.wait_ge(q_past_ready, h)
                    act.wait_ge(states_ready, h)
                for c in range(NC + 1):
                    source = X[:, 2, CH[c]] if c < NC else X[:, 3, 0:TS]
                    last = nc.scalar.activation(past[:, CH[c]], source, ACT.Exp, bias=m_prev_all[:, h, c:c + 1])
                last.then_inc(past_ready, 1)

            split_hi(0, U_IN + 1, 0)
            root(1)
            split_hi(0, U_IN + 2, 0)
            act.wait_ge(gates_biased, 1)
            link(nc.scalar.activation(rows[:, E_ROW, :], rows[:, F_ROW, :], ACT.Abs))
            link(nc.scalar.activation(rows[:, LF_ROW, :], rows[:, E_ROW, :], ACT.Exp, scale=-1.0))
            nc.scalar.activation(rows[:, E_ROW, :], rows[:, LF_ROW, :], ACT.Ln, bias=ones[0:H, 0:1]).then_inc(gates_ln, 1)
            for h in range(2 * H):
                for u in range(4):
                    if h or u:
                        split_hi(0, U_IN + 4 * h + u + 2, 0)
                    if h and u == 0:
                        step_gate(h - 1)
                    if h and u == 1:
                        step_o(h - 1)
                    if h == 0 and u == 1:
                        act.wait_ge(gate_cols_moved, 1)
                        act.wait_ge(mixer_consts, 1)
                        cols = X[:, 2, 0:(NC + 1) * 64].rearrange("p (c q) -> p c q", q=64)
                        nc.scalar.activation(key_col[:, 0:NC, :], cols[:, 0:NC, 0:H], ACT.Copy)
                        nc.scalar.activation(key_col[0:TS, NC, :], cols[0:TS, NC, 0:H], ACT.Copy)
                        nc.scalar.activation(neg_m_exp[:, 0:NC, :], cols[:, 0:NC, 32:32 + H], ACT.Exp)
                        nc.scalar.activation(neg_m_exp[0:TS, NC, :], cols[0:TS, NC, 32:32 + H], ACT.Exp)
                        nc.scalar.activation(m_prev_all[:, :, :], X[:, 3, 0:H * (NC + 1)].rearrange("p (h c) -> p h c", h=H),
                                             ACT.Copy).then_inc(gate_cols_ready, 1)
                        act.wait_ge(gate_cols_ready, 1)
                    if u == 2 and h < H:
                        step_weights(h)
                    if u == 2 and h:
                        step_y(h - 1)
                    if u == 3:
                        step_values(h)
            for step in (step_gate, step_o, step_y):
                step(2 * H - 1)
            for j in range(DT):
                split_hi(0, U_OUT + j + 2, 0)
                normed_hi(0, j, T_OUT + j, G_FFN2, 0)
                square(j, 2)

            ffn(1, U_F2, T_F2, U_D2, T_D2, 2)

            act.wait_ge(final_sums, 1)
            nc.scalar.activation(rms_tok[:, 0, 0:NC], X[:, 0, 0:NC], ACT.Sqrt, scale=1.0 / D, bias=eps[:, :])
            nc.scalar.activation(rms_tok[0:TS, 0, NC:NC + 1], X[0:TS, 0, NC:NC + 1], ACT.Sqrt, scale=1.0 / D,
                                 bias=eps[0:TS, :]).then_inc(final_root, 1)
            act.wait_ge(final_rstd, 1)
            for c in (1, 3):
                nc.scalar.activation(y_tok[:, c, :], y_tok[:, c, :], ACT.Copy, scale=rms_tok[:, 1, c:c + 1])\
                    .then_inc(y_done[c], 1)

        @block.vector
        def _(dve):
            link = chained(dve, dve_step)

            def split_lo(i, s, step):
                if s >= U_END:
                    return
                dve.wait_ge(w_hi_ready, s + 1 + step * i)
                if s == U_GATE:
                    for n in range(2):
                        last = nc.vector.tensor_tensor(w_lo[:, s % 4, :, 32 * n:32 * n + H], w_gates[:, :, H * n:H * (n + 1)],
                                                       w_hi[:, s % 4, :, 32 * n:32 * n + H].bitcast(F32), ALU.subtract)
                    last.then_inc(w_lo_ready, 1)
                    return
                nk = k_tiles(s)
                nc.vector.tensor_tensor(w_lo[:, s % 4, 0:nk, :], w_raw[:, s % 2, 0:nk, :],
                                        w_hi[:, s % 4, 0:nk, :].bitcast(F32), ALU.subtract).then_inc(w_lo_ready, 1)

            def normed_lo(i, j, norm, g, step):
                dve.wait_ge(xg_hi_ready, DT * norm + j + 1 + step * i)
                nc.vector.scalar_tensor_tensor(
                    xg_lo[:, j + step * i, :], xT[:, j + step * i, :], gains[:, bass.ds(g + j + step * i, 1)],
                    xg_hi[:, j + step * i, :].bitcast(F32), ALU.mult, ALU.subtract).then_inc(xg_lo_ready, 1)

            def invert_root(n):
                dve.wait_ge(norm_root, n + 1)
                nc.vector.reciprocal(rstd[:, :], rstd[:, :]).then_inc(rstd_ready, 1)
                dve.wait_ge(rstd_ready, n + 1)

            def take_out(i, j):
                dve.wait_ge(out_turned, j + 1 + 2 * i)
                b = 2 * (j % 2)
                cols = bass.ds((j + 2 * i) * P, P)
                nc.vector.tensor_copy(y_tok[:, 0:NC, cols], X[:, b, :].rearrange("p (c d) -> p c d", c=NC))
                nc.vector.tensor_copy(y_tok[0:TS, NC, cols], X[0:TS, b + 1, 0:P]).then_inc(out_taken, 1)

            def ffn(n, u_base, t_base, d_base, td_base, norm):
                def gate_up(i, s, g):
                    for u in range(4):
                        split_lo(i, s + u + 2, 4)
                        t = t_base + s - u_base + u
                        j = 2 * g + u // 2
                        if g == 0 and u == 0:
                            invert_root(norm)
                        dve.wait_ge(unit_done, s + u + 1 + 4 * i)
                        if u % 2 == 0:
                            if n or j:
                                dve.wait_ge(silu_ready, FT * n + j + 2 * i)
                            nc.vector.tensor_tensor(split_cols(gate_n[:, :]), halves(dense[t % 2]), split_cols(rstd[:, :]),
                                                    ALU.mult).then_inc(evicted, 1)
                        else:
                            dve.wait_ge(silu_scaled, FT * n + j + 1 + 2 * i)
                            if n or j:
                                dve.wait_ge(h_lo_ready, FT * n + j + 2 * i)
                            nc.vector.tensor_tensor(split_cols(h_f[:, :]), halves(dense[t % 2]), split_cols(gate_r[:, :]),
                                                    ALU.mult).then_inc(evicted, 1)

                groups(dve, u_base, 2 * FT, 4, gate_up)

                def down(i, s, g):
                    for v in range(2):
                        for u in range(4):
                            split_lo(i, s + 4 * v + u + 2, 8)
                        j = 2 * g + v
                        add_residual(s + 4 * v + 3, 8, i, j, td_base + j, 0.5, 2)
                        dve.wait_ge(evicted, td_base + j + 1 + 2 * i)
                        dve.wait_ge(sq_added, DT * (norm + 1) + j + 2 * i)
                        nc.vector.tensor_tensor(sq[:, :], xT[:, j + 2 * i, :], xT[:, j + 2 * i, :], ALU.mult).then_inc(sq_ready, 1)
                        if n == 0:
                            normed_lo(i, j, 1, G_MIX, 2)
                        elif not (g == 0 and v == 0):
                            take_out(i, j - 1)

                groups(dve, d_base, 4 * DT, 8, down)

            def add_residual(s, unit_step, i, j, t, factor, step):
                dve.wait_ge(unit_done, s + 1 + unit_step * i)
                x = split_cols(xT[:, j + step * i, :])
                nc.vector.scalar_tensor_tensor(x, halves(dense[t % 2]), factor, x, ALU.mult, ALU.add).then_inc(evicted, 1)

            def take_x(j):
                dve.wait_ge(x_moved, j + 1)
                nc.vector.tensor_copy(xT[:, j, :], dense[j % 2][:, :, :].rearrange("p a b -> p (a b)")[:, 0:T]).then_inc(evicted, 1)

            take_x(0)
            for j in range(DT):
                if j + 1 < DT:
                    take_x(j + 1)
                normed_lo(0, j, 0, G_FFN1, 0)
                if j in (3, 6):
                    split_lo(0, j // 3 - 1, 0)

            ffn(0, U_F1, T_F1, U_D1, T_D1, 0)

            def take(t, out, scale=None):
                if scale is None:
                    return nc.vector.tensor_tensor(split_cols(out), halves(dense[t % 2]), split_cols(rstd[:, :]), ALU.mult)
                return nc.vector.scalar_tensor_tensor(split_cols(out), halves(dense[t % 2]), scale, split_cols(rstd[:, :]),
                                                      ALU.mult, ALU.mult)

            def take_rotated(t, n):
                if n:
                    dve.wait_ge(rotated, n)
                else:
                    dve.wait_ge(tables_scaled, 1)
                tile = halves(dense[t % 2])
                nc.vector.tensor_tensor(split_cols(rot[:, 0, :]), tile, split_cols(table[:, COS:COS + T]), ALU.mult)
                for a, b in ((0, 64), (64, 0)):
                    last = nc.vector.tensor_tensor(split_cols(rot[a:a + 64, 1, :]), tile[b:b + 64],
                                                   split_cols(table[b:b + 64, SIN:SIN + T]), ALU.mult)
                last.then_inc(evicted, 1)

            def gate_rows_start():
                dve.wait_ge(unit_done, U_GATE + 1)
                tile = halves(dense[T_GATE % 2])
                nc.vector.tensor_tensor(split_cols(rows[:, I_ROW, :]), tile[0:H], split_cols(rstd[0:H, :]), ALU.mult)
                nc.vector.tensor_tensor(split_cols(rows[:, F_ROW, :]), tile[32:32 + H], split_cols(rstd[32:32 + H, :]), ALU.mult)\
                    .then_inc(evicted, 1)
                dve.wait_ge(evicted, T_GATE + 1)
                dve.wait_ge(gates_loaded, 16 * 4)
                nc.vector.tensor_scalar(rows[:, I_ROW, :], rows[:, I_ROW, :], row_small[:, 0:1], None, ALU.add)
                nc.vector.tensor_scalar(rows[:, F_ROW, :], rows[:, F_ROW, :], row_small[:, 1:2], None, ALU.add)\
                    .then_inc(gates_biased, 1)

            def gate_rows_end():
                dve.wait_ge(gates_ln, 1)
                r = lambda n, cols=slice(0, T): rows[:, n, cols]
                link(nc.vector.scalar_tensor_tensor(r(LF_ROW), r(F_ROW), 0.0, r(E_ROW), ALU.min, ALU.subtract))
                nc.vector.tensor_tensor_scan(r(M_ROW, slice(0, TP)), r(LF_ROW, slice(0, TP)), r(I_ROW, slice(0, TP)), 0.0,
                                             ALU.add, ALU.max)
                nc.vector.tensor_tensor_scan(r(M_ROW, CH[NC]), r(LF_ROW, CH[NC]), r(I_ROW, CH[NC]), row_small[:, 2:3],
                                             ALU.add, ALU.max)
                for c in range(NC + 1):
                    n = P if c < NC else TS
                    last = nc.vector.tensor_tensor_scan(r(B_ROW, CH[c]), ones[0:H, 0:n], r(LF_ROW, CH[c]), 0.0, ALU.mult, ALU.add)
                link(last)
                dve.wait_ge(mixer_consts, 1)
                nc.vector.tensor_tensor(r(BM_ROW), r(B_ROW), r(M_ROW), ALU.subtract)
                nc.vector.tensor_tensor(row_cols[0:H, :], r(I_ROW), r(B_ROW), ALU.subtract)
                nc.vector.tensor_scalar(row_cols[32:32 + H, :], r(M_ROW), -1.0, None, ALU.mult)
                nc.vector.tensor_scalar(row_small[:, M_PREV:M_PREV + 1], row_small[:, 2:3], 0.0, None, ALU.mult)
                nc.vector.tensor_copy(row_small[:, M_PREV + 1:M_PREV + NC], rows[:, M_ROW, P - 1:TP - 1:P])
                nc.vector.tensor_copy(row_small[:, M_OUT:M_OUT + 1], rows[:, M_ROW, TP - 1:TP])
                nc.vector.tensor_copy(row_small[:, M_OUT + 1:M_OUT + 2], rows[:, M_ROW, T - 1:T])
                nc.vector.tensor_copy(row_small[:, M_PREV + NC:M_PREV + NC + 1], row_small[:, 2:3]).then_inc(gate_rows_ready, 1)

            def step_scores(h):
                dve.wait_ge(scores_done, h + 1)
                if h:
                    dve.wait_ge(mixed_done, h)
                grid = lambda ap: ap.rearrange("p (c d) -> p c d", c=NC)
                if h < H:
                    dve.wait_ge(weights_ready, h + 1)
                    nc.vector.tensor_tensor(scores[:, 0:TP], X[:, 3, :], weights[:, 0:TP], ALU.mult)
                    nc.vector.tensor_tensor(scores[0:TS, TP:T], X[0:TS, 2, 2 * P:2 * P + TS], weights[0:TS, TP:T], ALU.mult)
                    keep = grid(weights[:, 0:TP])[:, :, P - 1:P].broadcast_to([P, NC, P])
                    nc.vector.tensor_tensor(k_tail[:, 0:NC, :], grid(X[:, 0, :]), keep, ALU.mult)
                    nc.vector.tensor_scalar(k_tail[0:TS, NC, :], X[0:TS, 2, 0:P], weights[0:TS, T - 1:T], None, ALU.mult)
                else:
                    d = DECAY + (h - H) * P
                    decay = table[:, d:d + P].rearrange("p (c d) -> p c d", c=1)
                    nc.vector.tensor_tensor(grid(scores[:, 0:TP]), grid(X[:, 3, :]), decay.broadcast_to([P, NC, P]), ALU.mult)
                    nc.vector.tensor_tensor(scores[0:TS, TP:T], X[0:TS, 2, 2 * P:2 * P + TS], table[0:TS, d:d + TS], ALU.mult)
                    nc.vector.tensor_scalar(k_tail[0:TS, NC, :], X[0:TS, 2, 0:P],
                                            table[0:TS, TAIL_S + h - H:TAIL_S + h - H + 1], None, ALU.mult)
                nc.vector.tensor_copy(v_tok[0:TS, NC, 0:P], X[0:TS, 2, P:2 * P]).then_inc(scores_weighted, 1)

            def step_states(h):
                dve.wait_ge(updates_done, h + 1)
                if h == 0:
                    dve.wait_ge(state_loaded, 16 * (2 + H))
                add = lambda c: X[:, 0 if c < 3 else 1, (c % 3) * V1:(c % 3 + 1) * V1]

                def kept(c, n):
                    if h < H:
                        return past[:, CH[c].stop - 1:CH[c].stop]
                    return float(np.exp(LOG_GAMMA[h - H] * np.float32(n)))

                sample_in = state_in[:, h, :]
                nc.vector.scalar_tensor_tensor(state_s[:, h, :], sample_in, kept(NC, TS), X[:, 1, V1:2 * V1], ALU.mult, ALU.add)
                link(nc.vector.tensor_copy(chain[:, 0, :], add(0)))
                for c in range(1, NC):
                    out = chain[:, c, :] if c < NC - 1 else state_p[:, h, :]
                    last = nc.vector.scalar_tensor_tensor(out, chain[:, c - 1, :], kept(c, P), add(c), ALU.mult, ALU.add)
                    if c < NC - 1:
                        link(last)
                last.then_inc(states_ready, 1)

            def step_norm(h):
                dve.wait_ge(o_ready, h + 1)
                for c in range(NC + 1):
                    n = P if c < NC else TS
                    last = nc.vector.bn_stats(stats[0:n, c, :], o_tok[0:n, c, 0:P])
                link(last)
                for c in range(NC + 1):
                    n = P if c < NC else TS
                    last = nc.vector.bn_aggr(mean_var[0:n, c, :], stats[0:n, c, :])
                link(last)
                den, inv, var, root, scale, shift = (small[:, k, :] for k in range(6))
                if h < H:
                    link(nc.vector.scalar_tensor_tensor(den, o_tok[:, :, P], -1.0, o_tok[:, :, P], ALU.mult, ALU.max))
                    link(nc.vector.tensor_tensor(den, den, neg_m_exp[:, :, h], ALU.max))
                    link(nc.vector.reciprocal(inv, den))
                    link(nc.vector.tensor_tensor(var, mean_var[:, :, 1], inv, ALU.mult))
                    nc.vector.tensor_tensor(var, var, inv, ALU.mult).then_inc(var_ready, 1)
                    dve.wait_ge(root_ready, h + 1)
                    link(nc.vector.tensor_tensor(scale, root, inv, ALU.mult))
                else:
                    nc.vector.tensor_copy(var, mean_var[:, :, 1]).then_inc(var_ready, 1)
                    dve.wait_ge(root_ready, h + 1)
                    link(nc.vector.tensor_copy(scale, root))
                nc.vector.scalar_tensor_tensor(shift, mean_var[:, :, 0], -1.0, scale, ALU.mult, ALU.mult).then_inc(shift_ready, 1)
                dve.wait_ge(shift_ready, h + 1)
                for c in range(NC - 1):
                    n = P if c < NC else TS
                    last = nc.vector.tensor_scalar(o_tok[0:n, c, 0:P], o_tok[0:n, c, 0:P], scale[0:n, c:c + 1], shift[0:n, c:c + 1],
                                                   ALU.mult, ALU.add)
                last.then_inc(normed, 1)

            def step_y(h):
                dve.wait_ge(turned, h + 1)
                dve.wait_ge(gate_act_ready, h + 1)
                if h:
                    dve.wait_ge(y_lo_ready, h)
                flat = X[:, 0:2, :].rearrange("p a b -> p (a b)")
                nc.vector.scalar_tensor_tensor(y_f[:, :], flat[:, 0:T], gains[:, G_GN + h:G_GN + h + 1], gate_act[:, :],
                                               ALU.mult, ALU.mult).then_inc(y_ready, 1)

            def step_arg(h):
                dve.wait_ge(rows_spread, h + 1)
                if h:
                    dve.wait_ge(weights_ready, h)
                grid = lambda ap: ap.rearrange("p (c d) -> p c d", c=NC)
                m = mask[:, :].rearrange("p (c d) -> p c d", c=1).broadcast_to([P, NC, P])
                nc.vector.tensor_tensor(grid(weights_arg[:, 0:TP]), grid(X[:, 2, :]), m, ALU.add)
                nc.vector.tensor_tensor(weights_arg[0:TS, TP:T], X[0:TS, 3, 0:TS], mask[0:TS, 0:TS], ALU.add).then_inc(arg_ready, 1)

            split_lo(0, U_IN + 1, 0)
            invert_root(1)
            gate_rows_start()
            for h in range(2 * H):
                for u in range(4):
                    s, t = U_IN + 4 * h + u, T_IN + 4 * h + u
                    split_lo(0, s + 2, 0)
                    dve.wait_ge(unit_done, s + 1)
                    if h >= 2:
                        dve.wait_ge(gate_act_ready, h - 1)
                        dve.wait_ge(scores_done, h - 1)
                        dve.wait_ge(q_past_ready, h - 1)
                    if h >= H and u < 2:
                        take_rotated(t, 2 * (h - H) + u)
                    else:
                        take(t, proj[:, h % 2, u, :], P ** -0.5 if u == 1 else None).then_inc(evicted, 1)
                    if h == 0 and u == 0:
                        gate_rows_end()
                    if u == 2 and h < H:
                        step_arg(h)
                    if u == 3:
                        step_scores(h)
                    elif h:
                        (step_states, step_norm, step_y)[u](h - 1)
            for step in (step_states, step_norm, step_y):
                step(2 * H - 1)
            for j in range(DT):
                split_lo(0, U_OUT + j + 2, 0)
                add_residual(U_OUT + j, 0, 0, j, T_OUT + j, 1.0, 0)
                normed_lo(0, j, 2, G_FFN2, 0)

            ffn(1, U_F2, T_F2, U_D2, T_D2, 2)
            take_out(0, DT - 1)
            dve.wait_ge(final_root, 1)
            nc.vector.reciprocal(rms_tok[:, 1, 0:NC], rms_tok[:, 0, 0:NC])
            nc.vector.reciprocal(rms_tok[0:TS, 1, NC:NC + 1], rms_tok[0:TS, 0, NC:NC + 1]).then_inc(final_rstd, 1)
            dve.wait_ge(final_rstd, 1)
            dve.wait_ge(out_taken, DT)
            for c in (0, 2, NC):
                n = P if c < NC else TS
                nc.vector.tensor_scalar(y_tok[0:n, c, :], y_tok[0:n, c, :], rms_tok[0:n, 1, c:c + 1], None, ALU.mult)\
                    .then_inc(y_done[c], 1)

        @block.gpsimd
        def _(pool):
            link = chained(pool, pool_step)

            def triangle(ap, pattern, op, fill, base=0, mult=1):
                return nc.gpsimd.affine_select(out=ap, in_=ap, compare_op=op, fill=fill, base=base, pattern=pattern,
                                               channel_multiplier=mult)

            link(nc.gpsimd.memset(ident[:, :], 0.0))
            triangle(ident[:, :], [[-1, P]], ALU.not_equal, 1.0).then_inc(consts_ready, 1)
            nc.gpsimd.memset(ones[:, :], 1.0).then_inc(consts_ready, 1)
            nc.gpsimd.memset(eps[:, :], EPS).then_inc(consts_ready, 1)

            def add_square(i, j, norm, step, reset=False):
                if reset:
                    if norm:
                        pool.wait_ge(norm_sums, norm)
                    link(nc.gpsimd.memset(sq_sum[:, :], 0.0))
                pool.wait_ge(sq_ready, DT * norm + j + 1 + step * i)
                if not reset:
                    pool.wait_ge(sq_added, DT * norm + j + step * i)
                nc.gpsimd.tensor_tensor(sq_sum[:, :], sq_sum[:, :], sq[:, :], ALU.add).then_inc(sq_added, 1)

            def ffn(n, u_base, norm):
                def gate_up(i, s, g):
                    for v in range(2):
                        j = 2 * g + v
                        if g == 0 and v == 0:
                            pool.wait_ge(rstd_ready, norm + 1)
                        pool.wait_ge(silu_ready, FT * n + j + 1 + 2 * i)
                        nc.gpsimd.tensor_tensor(gate_r[:, :], gate_s[:, :], rstd[:, :], ALU.mult).then_inc(silu_scaled, 1)
                        pool.wait_ge(h_hi_ready, FT * n + j + 1 + 2 * i)
                        nc.gpsimd.tensor_tensor(h_lo[:, j + 2 * i, :], h_f[:, :], h_hi[:, j + 2 * i, :].bitcast(F32),
                                                ALU.subtract).then_inc(h_lo_ready, 1)

                groups(pool, u_base, 2 * FT, 4, gate_up)

                def down(i, s, g):
                    for v in range(2):
                        add_square(i, 2 * g + v, norm + 1, 2, reset=g == 0 and v == 0)
                        if n == 0 and g == DT // 2 - 1 and v == 0:
                            pool.wait_ge(unit_done, U_GATE - 3)
                            nc.gpsimd.memset(w_hi[:, U_GATE % 4, :, :].bitcast(F32), 0.0).then_inc(gate_slots_zeroed, 1)
                            nc.gpsimd.memset(w_lo[:, U_GATE % 4, :, :].bitcast(F32), 0.0).then_inc(gate_slots_zeroed, 1)

                groups(pool, u_base + 2 * FT, 4 * DT, 8, down)

            for j in range(DT):
                add_square(0, j, 0, 0, reset=j == 0)
            ffn(0, U_F1, 0)

            pool.wait_ge(unit_done, U_GATE)
            link(nc.gpsimd.memset(mask[:, :], 0.0))
            link(triangle(mask[:, :], [[1, P]], ALU.is_ge, -1e30, mult=-1))
            link(nc.gpsimd.memset(sel[:, :, :], 1.0))
            link(triangle(sel[:, :, :], [[-1, H], [0, P]], ALU.is_equal, 0.0))
            nc.gpsimd.memset(row_cols[:, :], 0.0)
            nc.gpsimd.memset(neg_m_exp[:, :, :], 1.0)
            nc.gpsimd.memset(v_tok[:, :, P:V1], 1.0)
            nc.gpsimd.memset(o_tok[:, NC, :], 1.0)
            nc.gpsimd.memset(mean_var[:, :, :], 0.0)
            nc.gpsimd.memset(small[:, 6, :], -0.5)
            nc.gpsimd.memset(state_in[:, H:2 * H, P:V1], 0.0).then_inc(mixer_consts, 1)

            def step_q_past(h):
                if h < H:
                    pool.wait_ge(past_ready, h + 1)
                    pool.wait_ge(evicted, T_IN + 4 * h + 1)
                else:
                    pool.wait_ge(rotated, 2 * (h - H) + 1)
                if h:
                    pool.wait_ge(mixed_done, h)
                if h < H:
                    nc.gpsimd.tensor_tensor(q_past[:, :], proj[:, h % 2, 0, :], past[:, :], ALU.mult).then_inc(q_past_ready, 1)
                    return
                grid = lambda ap: ap.rearrange("p (c d) -> p c d", c=NC)
                d = CROSS + (h - H) * P
                cross = table[:, d:d + P].rearrange("p (c d) -> p c d", c=1).broadcast_to([P, NC, P])
                nc.gpsimd.tensor_tensor(grid(q_past[:, 0:TP]), grid(proj[:, h % 2, 0, 0:TP]), cross, ALU.mult)
                nc.gpsimd.tensor_tensor(q_past[:, TP:T], proj[:, h % 2, 0, TP:T], table[:, d:d + TS], ALU.mult)\
                    .then_inc(q_past_ready, 1)

            def step_root(h):
                pool.wait_ge(var_ready, h + 1)
                link(nc.gpsimd.tensor_scalar(small[:, 7, :], small[:, 2, :], GN_EPS, None, ALU.add))
                nc.gpsimd.tensor_tensor(small[:, 3, :], small[:, 7, :], small[:, 6, :], ALU.pow).then_inc(root_ready, 1)

            def step_y_lo(h):
                pool.wait_ge(y_hi_ready, h + 1)
                nc.gpsimd.tensor_tensor(y_lo(h), y_f[:, :], y_hi(h).bitcast(F32), ALU.subtract).then_inc(y_lo_ready, 1)

            for h in range(2 * H):
                for u in range(4):
                    if h >= H and u < 2:
                        pool.wait_ge(evicted, T_IN + 4 * h + u + 1)
                        nc.gpsimd.tensor_tensor(proj[:, h % 2, u, :], rot[:, 0, :], rot[:, 1, :], ALU.add).then_inc(rotated, 1)
                    if h == 1 and u == 3:
                        pool.wait_ge(table_loaded, 16)
                        pool.wait_ge(rstd_ready, 2)
                        nc.gpsimd.tensor_tensor(table[:, COS:COS + T], table[:, COS:COS + T], rstd[:, :], ALU.mult)
                        nc.gpsimd.tensor_tensor(table[:, SIN:SIN + T], table[:, SIN:SIN + T], rstd[:, :], ALU.mult)\
                            .then_inc(tables_scaled, 1)
                    if h and u == 1:
                        step_root(h - 1)
                    if u == 2:
                        step_q_past(h)
                        if h:
                            step_y_lo(h - 1)
            step_root(2 * H - 1)
            step_y_lo(2 * H - 1)
            for j in range(DT):
                add_square(0, j, 2, 0, reset=j == 0)

            ffn(1, U_F2, 2)


_INS = ['x_prompt', 'x_sample', 'state_mlstm_C', 'state_mlstm_n', 'state_mlstm_m', 'state_ret_R', 'g_ffn1',
        'w_ffn1_gate', 'w_ffn1_up', 'w_ffn1_down', 'g_mix', 'w_in', 'b_gates', 'g_gn_mlstm', 'g_gn_ret', 'w_out',
        'g_ffn2', 'w_ffn2_gate', 'w_ffn2_up', 'w_ffn2_down', 'g_final']


def kernel(**inputs):
    import numpy as _np
    import concourse.bacc as _bacc
    from concourse import mybir as _mybir
    from concourse.bass_utils import run_bass_kernel_spmd as _run

    xp, xs = inputs['x_prompt'].shape, inputs['x_sample'].shape
    state, norm = (1, 1, H, P, P), (1, 1, H, P)
    outs = [xp, xs] + 2 * [state, norm, (1, 1, H), state]
    nc = _bacc.Bacc("TRN2", target_bir_lowering=False, num_devices=1)
    arrays, args = {}, []
    for name in _INS:
        arrays[f"in_{name}"] = _np.ascontiguousarray(inputs[name])
    arrays["in_tables"] = shape_tables(xp[1], xs[1])
    for name, a in arrays.items():
        args.append(nc.dram_tensor(name, a.shape, _mybir.dt.from_np(a.dtype), kind="ExternalInput").ap())
    for i, shape in enumerate(outs):
        args.append(nc.dram_tensor(f"out_{i}", shape, _mybir.dt.float32, kind="ExternalOutput").ap())
    hybrid_trunk_step(nc, *args)
    r = _run(nc, [arrays], core_ids=[0])
    return tuple(r.results[0][f"out_{i}"] for i in range(len(outs)))
```

```python
from contextlib import ExitStack

import numpy as np

import concourse.bass as bass
from concourse import mybir

ALU = mybir.AluOpType
ACT = mybir.ActivationFunctionType
F32 = mybir.dt.float32
F32R = mybir.dt.float32r

P = 128
H = 4
EPS = 1e-6
GN_EPS = 1e-5
PAST_LEN = 1024
ROPE_BASE = 10000.0

LOG_GAMMA = np.log(1.0 - 2.0 ** (-5.0 - np.arange(H))).astype(np.float32)


def shape_tables(tp, ts):
    t = tp + ts
    half = P // 2
    inv = (np.float32(ROPE_BASE) ** (-np.arange(half, dtype=np.float32) / half)).astype(np.float32)
    pos = np.concatenate([np.arange(tp), PAST_LEN + np.arange(ts)]).astype(np.float32)
    ang = inv[:, None] * pos[None, :]
    cos = np.cos(ang).astype(np.float32)
    sin = np.sin(ang).astype(np.float32)
    idx = np.arange(P, dtype=np.float32)
    diff = idx[None, :] - idx[:, None]
    scale = np.float32(P ** -0.5)
    decay = [np.where(diff >= 0, np.exp(lg * np.maximum(diff, 0)), 0).astype(np.float32) * scale for lg in LOG_GAMMA]
    cross = [np.broadcast_to(np.exp(lg * (idx + 1)), (P, P)) for lg in LOG_GAMMA]
    tail = np.stack([np.exp(lg * (P - 1 - idx)) * scale for lg in LOG_GAMMA], 1)
    tail_s = np.stack([np.exp(lg * np.maximum(ts - 1 - idx, 0)) * scale for lg in LOG_GAMMA], 1)
    cols = [np.concatenate([cos, cos]), np.concatenate([sin, -sin]), *decay, *cross, tail, tail_s]
    table = np.ascontiguousarray(np.concatenate(cols, axis=1).astype(np.float32))
    assert table.shape == (P, 2 * t + 8 * P + 8)
    return table


def hybrid_trunk_step(nc, x_prompt, x_sample, state_mlstm_C, state_mlstm_n, state_mlstm_m, state_ret_R,
                      g_ffn1, w_ffn1_gate, w_ffn1_up, w_ffn1_down, g_mix, w_in, b_gates, g_gn_mlstm, g_gn_ret,
                      w_out, g_ffn2, w_ffn2_gate, w_ffn2_up, w_ffn2_down, g_final, tables,
                      y_prompt, y_sample, C_prompt, n_prompt, m_prompt, R_prompt, C_sample, n_sample, m_sample,
                      R_sample):
    TP, D = x_prompt.shape[1], x_prompt.shape[2]
    TS = x_sample.shape[1]
    T = TP + TS
    TH = T // 2
    DT = D // P
    F = w_ffn1_gate.shape[2]
    FT = F // P
    NC = TP // P
    CH = [slice(c * P, (c + 1) * P) for c in range(NC)] + [slice(TP, T)]
    V1 = P + 1
    assert D == 8 * P and T % 2 == 0 and TH <= 512 and TP == 512 and TS == 32

    DOWN_K = [(0, 6), (6, 12), (12, 17), (17, FT)]
    U_F1 = 0
    U_D1 = U_F1 + 2 * FT
    U_GATE = U_D1 + 4 * DT
    U_IN = U_GATE + 1
    U_OUT = U_IN + 8 * H
    U_F2 = U_OUT + DT
    U_D2 = U_F2 + 2 * FT
    U_END = U_D2 + 4 * DT
    X_ORDER = (0, 1, NC, 2, 3)
    X_PIECES = [(c, half) for c in X_ORDER for half in ((0, 1) if c < NC else (0,))]
    LAST_CHUNKS = [(2, 3, NC), (0, 1)]
    LAST_COLS = [slice(2 * P, T), slice(0, 2 * P)]
    RAW = 4
    T_F1 = 0
    T_D1 = T_F1 + 2 * FT
    T_GATE = T_D1 + DT
    T_IN = T_GATE + 1
    T_OUT = T_IN + 8 * H
    T_F2 = T_OUT + DT
    T_D2 = T_F2 + 2 * FT

    def k_tiles(s):
        for base in (U_D1, U_D2):
            if base <= s < base + 4 * DT:
                a, b = DOWN_K[(s - base) % 4]
                return b - a
        return DT

    def groups(eng, base, count, step, body):
        n = count // step
        body(0, base, 0)
        with eng.Fori(0, n - 2) as i:
            body(i, base + step, 1)
        body(0, base + step * (n - 1), n - 1)

    with ExitStack() as ctx:
        at = {"next": -(-nc.sbuf_base // 32) * 32}

        def sb(name, shape, dt=F32):
            handle = nc.alloc_sbuf_tensor_at(name, shape, dt, offset=at["next"])
            at["next"] += -(-int(np.prod(shape[1:])) * 4 // 32) * 32
            return handle

        def sem(name):
            return ctx.enter_context(nc.semaphore(name))

        xT = sb("xT", [P, DT, T])
        w_raw = sb("w_raw", [P, RAW, DT, P])
        w_hi = sb("w_hi", [P, 4, DT, P], F32R)
        w_lo = sb("w_lo", [P, 4, DT, P], F32R)
        rstd = sb("rstd", [P, T])
        sq = sb("sq", [P, T])
        sq_sum = sb("sq_sum", [P, T])
        ident = sb("ident", [P, P])
        ones = sb("ones", [P, P])
        gains = sb("gains", [P, 5 * DT])
        eps = sb("eps", [P, 1])
        unused = sb("unused", [P, 1])
        w_gates = sb("w_gates", [P, DT, 2 * H])
        row_small = sb("row_small", [H, 16])
        G_FFN1, G_MIX, G_FFN2, G_FINAL, G_GN = (DT * n for n in range(5))

        xg_region = at["next"]
        xg_hi = sb("xg_hi", [P, DT, T], F32R)
        xg_lo = sb("xg_lo", [P, DT, T], F32R)
        xg_end = at["next"]
        at["next"] = xg_region
        y_tok = sb("y_tok", [P, NC + 1, D])
        x_gain = sb("x_gain", [P, 2, T])
        rms_tok = sb("rms_tok", [P, 2, NC + 1])
        assert at["next"] <= xg_end

        at["next"] = stage_region = xg_end
        x_tok = sb("x_tok", [P, NC + 1, D])
        gain_rows = sb("gain_rows", [5 * DT, P])
        x_squared = sb("x_squared", [P, D])
        x_sums = sb("x_sums", [P, NC + 1])

        at["next"] = stage_region
        h_hi = sb("h_hi", [P, FT, T], F32R)
        h_lo = sb("h_lo", [P, FT, T], F32R)
        gate_n = sq
        gate_s = sb("gate_s", [P, T])
        gate_r = sb("gate_r", [P, T])
        h_f = sb("h_f", [P, T])
        ffn_end = at["next"]

        at["next"] = stage_region
        y_hi_m = sb("y_hi_m", [P, H, T], F32R)
        y_lo_m = sb("y_lo_m", [P, H, T], F32R)
        y_ret_region = at["next"]
        y_hi_r = sb("y_hi_r", [P, H, T], F32R)
        y_lo_r = sb("y_lo_r", [P, H, T], F32R)
        y_ret_end = at["next"]
        at["next"] = y_ret_region
        rows = sb("rows", [H, 5, T])
        row_cols = sb("row_cols", [64, T])
        sel = sb("sel", [H, H, P])
        assert at["next"] <= y_ret_end
        at["next"] = y_ret_end
        proj = sb("proj", [P, 2, 4, T])
        table = sb("table", [P, tables.shape[1]])
        sel_r = sb("sel_r", [H, H, P], F32R)
        bm_split = sb("bm_split", [H, 2, T], F32R)
        state_in = sb("state_in", [P, 2 * H, V1])
        state_p = sb("state_p", [P, 2 * H, V1])
        state_s = sb("state_s", [P, 2 * H, V1])
        chain = sb("chain", [P, NC - 1, V1])
        mlstm_only = at["next"]
        weights_arg = sb("weights_arg", [P, T])
        weights = sb("weights", [P, T])
        at["next"] = mlstm_only
        rot = sb("rot", [P, 2, T])
        past = sb("past", [P, T])
        q_past = sq_sum
        scores = sb("scores", [P, T])
        k_tail = sb("k_tail", [P, NC + 1, P])
        v_tok = sb("v_tok", [P, NC + 1, V1])
        o_tok = sb("o_tok", [P, NC + 1, P])
        gate_act = sb("gate_act", [P, T])
        y_f = sb("y_f", [P, T])
        mask = sb("mask", [P, P])
        key_col = sb("key_col", [P, NC + 1, H])
        neg_m_exp = sb("neg_m_exp", [P, NC + 1, H])
        m_prev_all = sb("m_prev_all", [P, H, NC + 1])
        stats = sb("stats", [P, NC + 1, 6])
        mean_var = sb("mean_var", [P, NC + 1, 2])
        small = sb("small", [P, 7, NC + 1])
        mixer_end = at["next"]
        at["next"] = max(ffn_end, mixer_end)
        assert at["next"] <= nc.sbuf_usable_end, (at["next"], nc.sbuf_usable_end, ffn_end, mixer_end)

        I_ROW, F_ROW, E_ROW, LF_ROW, M_ROW = range(5)
        B_ROW, BM_ROW = F_ROW, E_ROW
        M_PREV, M_OUT = 4, 9
        ACT_CHUNKS = (NC - 1, NC)
        COS, SIN, DECAY, CROSS = 0, T, 2 * T, 2 * T + H * P
        TAIL, TAIL_S = CROSS + H * P, CROSS + H * P + H

        dense = [ctx.enter_context(nc.psum_tensor(f"dense{n}", [P, 2, 512], F32)) for n in range(2)]
        X = ctx.enter_context(nc.psum_tensor("core_banks", [P, 4, 512], F32))

        def bank_of(t):
            return dense[(t - (t > T_OUT + 2)) % 2]

        def mixed(c, cols=slice(0, P)):
            b, o = (2, c) if c < 3 else (3, c - 3)
            return X[0:P if c < NC else TS, b, o * V1 + cols.start:o * V1 + cols.stop]

        def out_tile(j):
            return X[:, 2:4, :] if j == 2 else bank_of(T_OUT + j)

        def y_hi(kt):
            return (y_hi_m if kt < H else y_hi_r)[:, kt % H, :]

        def y_lo(kt):
            return (y_lo_m if kt < H else y_lo_r)[:, kt % H, :]

        def halves(tile):
            return tile[:, :, 0:TH]

        def split_cols(ap):
            return ap.rearrange("p (a b) -> p a b", a=2)

        x_loaded = [sem(f"x_loaded{c}") for c in range(NC + 1)]
        x_end_loaded = sem("x_end_loaded")
        gains_loaded = sem("gains_loaded")
        consts_ready = sem("consts_ready")
        gains_ready = sem("gains_ready")
        gains_moved = sem("gains_moved")
        w_loaded = [sem(f"w_loaded{n}") for n in range(RAW)]
        gates_loaded = sem("gates_loaded")
        gate_slots_zeroed = sem("gate_slots_zeroed")
        w_hi_ready = sem("w_hi_ready")
        w_lo_ready = sem("w_lo_ready")
        unit_done = sem("unit_done")
        x_moved = sem("x_moved")
        x_taken = sem("x_taken")
        x_summed = sem("x_summed")
        x_sums_spread = sem("x_sums_spread")
        evicted = sem("evicted")
        sq_ready = sem("sq_ready")
        sq_added = sem("sq_added")
        xg_hi_ready = sem("xg_hi_ready")
        xg_lo_ready = sem("xg_lo_ready")
        norm_sums = sem("norm_sums")
        norm_root = sem("norm_root")
        rstd_ready = sem("rstd_ready")
        silu_ready = sem("silu_ready")
        silu_scaled = sem("silu_scaled")
        h_hi_ready = sem("h_hi_ready")
        h_lo_ready = sem("h_lo_ready")
        table_loaded = sem("table_loaded")
        mixer_consts = sem("mixer_consts")
        state_loaded = sem("state_loaded")
        bm_hi_ready = sem("bm_hi_ready")
        bm_split_ready = sem("bm_split_ready")
        gates_biased = sem("gates_biased")
        gates_ln = sem("gates_ln")
        gate_rows_ready = sem("gate_rows_ready")
        gate_cols_moved = sem("gate_cols_moved")
        gate_cols_ready = sem("gate_cols_ready")
        tables_scaled = sem("tables_scaled")
        rotated = sem("rotated")
        rows_spread = sem("rows_spread")
        arg_ready = sem("arg_ready")
        weights_ready = sem("weights_ready")
        past_ready = sem("past_ready")
        q_past_ready = sem("q_past_ready")
        scores_done = sem("scores_done")
        scores_weighted = sem("scores_weighted")
        v_ready = sem("v_ready")
        gate_act_ready = sem("gate_act_ready")
        updates_done = sem("updates_done")
        states_ready = sem("states_ready")
        mixed_done = sem("mixed_done")
        var_ready = sem("var_ready")
        root_ready = sem("root_ready")
        shift_ready = sem("shift_ready")
        normed = sem("normed")
        normed_act = sem("normed_act")
        turned = sem("turned")
        y_ready = sem("y_ready")
        y_hi_ready = sem("y_hi_ready")
        y_lo_ready = sem("y_lo_ready")
        x_gained = sem("x_gained")
        out_turned = sem("out_turned")
        out_taken = sem("out_taken")
        last_part_done = sem("last_part_done")
        last_part_taken = sem("last_part_taken")
        final_sums = sem("final_sums")
        final_root = sem("final_root")
        final_rstd = sem("final_rstd")
        y_done = [sem(f"y_done{c}") for c in range(NC + 1)]
        stored = sem("stored")
        act_step = sem("act_step")
        dve_step = sem("dve_step")
        pool_step = sem("pool_step")

        def chained(eng, s):
            count = [0]

            def link(ins):
                count[0] += 1
                ins.then_inc(s, 1)
                eng.wait_ge(s, count[0])

            return link

        def w_rows(w):
            return w[0].rearrange("(k p) n -> p k n", p=P)

        block = ctx.enter_context(nc.Block())

        @block.sync
        def _(sp):
            def load_x(c):
                if c == NC - 1:
                    sp.dma_start(x_tok[:, c, 0:D // 2], x_prompt[0, CH[c], 0:D // 2]).then_inc(x_loaded[c], 16)
                    sp.dma_start(x_tok[:, c, D // 2:D], x_prompt[0, CH[c], D // 2:D]).then_inc(x_end_loaded, 16)
                elif c < NC:
                    sp.dma_start(x_tok[:, c, :], x_prompt[0, CH[c], :]).then_inc(x_loaded[c], 16)
                else:
                    sp.dma_start(x_tok[0:TS, c, :], x_sample[0, :, :]).then_inc(x_loaded[c], 16)

            load_x(0)
            load_x(1)
            load_x(NC)
            load_x(2)
            sp.dma_start(w_raw[:, 0, :, :], w_rows(w_ffn1_gate)[:, :, 0:P]).then_inc(w_loaded[0], 16)
            for n, g in enumerate((g_ffn1, g_mix, g_ffn2)):
                sp.dma_start(gain_rows[n * DT:(n + 1) * DT, :], g[0].rearrange("(k p) -> k p", p=P)).then_inc(gains_loaded, 16)
            sp.dma_start(gain_rows[G_FINAL:G_FINAL + DT, :], g_final.rearrange("(k p) -> k p", p=P)).then_inc(gains_loaded, 16)
            sp.dma_start(gain_rows[G_GN:G_GN + H, :], g_gn_mlstm[0].rearrange("(k p) -> k p", p=P)).then_inc(gains_loaded, 16)
            sp.dma_start(gain_rows[G_GN + H:G_GN + 2 * H, :], g_gn_ret[0].rearrange("(k p) -> k p", p=P)).then_inc(gains_loaded, 16)
            load_x(3)
            sp.dma_start(w_raw[:, 1, :, :], w_rows(w_ffn1_up)[:, :, 0:P]).then_inc(w_loaded[1], 16)

            sp.dma_start(row_small[:, 0:1], b_gates[0, 0:H].rearrange("(h a) -> h a", a=1)).then_inc(gates_loaded, 16)
            sp.dma_start(row_small[:, 1:2], b_gates[0, H:2 * H].rearrange("(h a) -> h a", a=1)).then_inc(gates_loaded, 16)
            sp.dma_start(row_small[:, 2:3], state_mlstm_m[0, 0].rearrange("(h a) -> h a", a=1)).then_inc(gates_loaded, 16)

            def load(i, s, step, source, nk):
                if s >= RAW:
                    sp.wait_ge(w_lo_ready, s - RAW + 1 + step * i)
                sp.dma_start(w_raw[:, s % RAW, 0:nk, :], source).then_inc(w_loaded[s % RAW], 16)

            def ffn(u_base, d_base, w_gate, w_up, w_down):
                gate_v, up_v, down_v = w_rows(w_gate), w_rows(w_up), w_rows(w_down)
                if u_base == 0:
                    for u in range(2, 4):
                        load(0, u, 0, (gate_v, up_v)[u % 2][:, :, (u // 2) * P:(u // 2 + 1) * P], DT)
                    sp.dma_start(w_gates[:, :, :], w_rows(w_in)[:, :, 8 * H * P:8 * H * P + 2 * H]).then_inc(gates_loaded, 16)
                with sp.Fori(0 if u_base else 1, FT // 2) as i:
                    for u in range(4):
                        w = (gate_v, up_v)[u % 2]
                        col = i * (2 * P) + (u // 2) * P
                        sp.wait_ge(w_lo_ready, u_base + u - RAW + 1 + 4 * i)
                        sp.dma_start(w_raw[:, (u_base + u) % RAW, :, :], w[:, :, bass.ds(col, P)])\
                          .then_inc(w_loaded[(u_base + u) % RAW], 16)
                with sp.Fori(0, DT) as i:
                    for u, (a, b) in enumerate(DOWN_K):
                        load(i, d_base + u, 4, down_v[:, a:b, bass.ds(i * P, P)], b - a)

            ffn(U_F1, U_D1, w_ffn1_gate, w_ffn1_up, w_ffn1_down)

            in_v = w_rows(w_in)
            for h in range(2 * H):
                for u in range(4):
                    col = (h // H) * 4 * H * P + u * H * P + (h % H) * P
                    load(0, U_IN + 4 * h + u, 0, in_v[:, :, col:col + P], DT)
                if h == 0:
                    sp.wait_ge(unit_done, U_GATE)
                    sp.dma_start(table[:, :], tables[:, :]).then_inc(table_loaded, 16)
                    sp.dma_start(state_in[:, 0:H, 0:P], state_mlstm_C[0, 0].rearrange("h d e -> d h e")).then_inc(state_loaded, 16)
                    sp.dma_start(state_in[:, H:2 * H, 0:P], state_ret_R[0, 0].rearrange("h d e -> d h e")).then_inc(state_loaded, 16)
                    for hh in range(H):
                        sp.dma_start(state_in[:, hh, P:V1], state_mlstm_n[0, 0, hh].rearrange("(d a) -> d a", a=1)).then_inc(state_loaded, 16)
            out_v = w_rows(w_out)
            for j in range(DT):
                load(0, U_OUT + j, 0, out_v[:, :, j * P:(j + 1) * P], DT)
            sp.wait_ge(states_ready, 2 * H)
            stores = 0
            for state, C_out, n_out, R_out in ((state_p, C_prompt, n_prompt, R_prompt), (state_s, C_sample, n_sample, R_sample)):
                sp.dma_start(C_out[0, 0].rearrange("h d e -> d h e"), state[:, 0:H, 0:P]).then_inc(stored, 16)
                sp.dma_start(R_out[0, 0].rearrange("h d e -> d h e"), state[:, H:2 * H, 0:P]).then_inc(stored, 16)
                for hh in range(H):
                    sp.dma_start(n_out[0, 0, hh].rearrange("(d a) -> d a", a=1), state[:, hh, P:V1]).then_inc(stored, 16)
                stores += 2 + H
            for out_m, t in ((m_prompt, M_OUT), (m_sample, M_OUT + 1)):
                sp.dma_start(out_m[0, 0].rearrange("(h a) -> h a", a=1), row_small[:, t:t + 1]).then_inc(stored, 16)
                stores += 1
            sp.wait_ge(stored, 16 * stores)

            ffn(U_F2, U_D2, w_ffn2_gate, w_ffn2_up, w_ffn2_down)

            for c in (2, 3, NC, 0, 1):
                sp.wait_ge(y_done[c], 1)
                if c < NC:
                    sp.dma_start(y_prompt[0, CH[c], :], y_tok[:, c, :]).then_inc(stored, 16)
                else:
                    sp.dma_start(y_sample[0, :, :], y_tok[0:TS, c, :]).then_inc(stored, 16)
            sp.wait_ge(stored, 16 * (stores + NC + 1))

        @block.tensor
        def _(pe):
            KEEP_WARM = 6

            def product(s, out, x_hi, x_lo, kts, start, stop, slot_k0=0, ready=None):
                for n, kt in enumerate(kts):
                    if ready is not None:
                        ready(kt)
                    k = kt - slot_k0
                    passes = [(w_hi, x_hi), (w_hi, x_lo), (w_lo, x_hi)]
                    for m, (w, x) in enumerate(passes):
                        for half in range(2):
                            last = nc.tensor.matmul(
                                out[:, half, 0:TH], w[:, s % 4, k, :], x(kt)[:, half * TH:(half + 1) * TH],
                                start=start and n == 0 and m == 0, stop=stop and n == len(kts) - 1 and m == 2)
                return last

            SUMS_K = (5, 5, 6)
            xg = (lambda kt: xg_hi[:, kt, :]), (lambda kt: xg_lo[:, kt, :])
            h_halves = (lambda kt: h_hi[:, kt, :]), (lambda kt: h_lo[:, kt, :])

            def tile_free(t, i=0, step=0):
                if t < 2:
                    pe.wait_ge(x_taken, len(X_PIECES) - 2 * (1 - t))
                    return
                pe.wait_ge(evicted, t - 1 + step * i)

            def norm_sums_of(n):
                if n:
                    pe.wait_ge(sq_added, DT * n)
                else:
                    pe.wait_ge(x_sums_spread, NC + 1)
                for half in range(2):
                    last = nc.tensor.matmul(X[:, half, 0:TH], ones[:, :], sq_sum[:, half * TH:(half + 1) * TH], start=True, stop=True)
                last.then_inc(norm_sums, 1)

            def xg_ready(n):
                return lambda kt: pe.wait_ge(xg_lo_ready, DT * n + kt + 1)

            def ffn(n, u_base, t_base, d_base, td_base, norm):
                def gate_up(i, s, g):
                    for u in range(4):
                        pe.wait_ge(w_lo_ready, s + u + 1 + 4 * i)
                        t = t_base + s - u_base + u
                        tile_free(t, i, 4)
                        first = g == 0 and u == 0
                        if first:
                            product(s, bank_of(t), *xg, range(SUMS_K[norm]), True, False, ready=xg_ready(norm))
                            if n:
                                pe.wait_ge(y_ready, 2 * H)
                            norm_sums_of(norm)
                            product(s, bank_of(t), *xg, range(SUMS_K[norm], DT), False, True, ready=xg_ready(norm))\
                                .then_inc(unit_done, 1)
                        else:
                            product(s + u, bank_of(t), *xg, range(DT), True, True).then_inc(unit_done, 1)

                groups(pe, u_base, 2 * FT, 4, gate_up)

                def down(i, s, g):
                    for v in range(2):
                        t = td_base + 2 * g + v
                        if n and 2 * g + v == DT - 1:
                            last_tile(s + 4 * v, t)
                            return
                        for u, (a, b) in enumerate(DOWN_K):
                            unit = s + 4 * v + u
                            pe.wait_ge(w_lo_ready, unit + 1 + 8 * i)
                            if u == 0:
                                tile_free(t, i, 2)
                            if g == 0 and v == 0:
                                pe.wait_ge(h_lo_ready, FT * n + b)
                            product(unit, bank_of(t), *h_halves, range(a, b), u == 0, u == 3, slot_k0=a).then_inc(unit_done, 1)
                            if n and u == 0 and not (g == 0 and v == 0):
                                turn_out(i, 2 * g + v - 1)

                groups(pe, d_base, 4 * DT, 8, down)

            def turn_out(i, j):
                pe.wait_ge(x_gained, j + 1 + 2 * i)
                b = 2 * (j % 2)
                if j >= 2:
                    pe.wait_ge(out_taken, j - 1 + 2 * i)
                for c in range(NC):
                    nc.tensor.transpose(X[:, b, CH[c]], x_gain[:, j % 2, CH[c]], ident[:, :])
                nc.tensor.transpose(X[0:TS, b + 1, 0:P], x_gain[:, j % 2, TP:T], ident[:, :]).then_inc(out_turned, 1)

            def last_tile(s, t):
                for part, cols in enumerate(LAST_COLS):
                    for u, (a, b) in enumerate(DOWN_K):
                        if part == 0:
                            pe.wait_ge(w_lo_ready, s + u + 1)
                            if u == 0:
                                tile_free(t)
                        for kt in range(a, b):
                            for m, (w, x) in enumerate(((w_hi, h_hi), (w_hi, h_lo), (w_lo, h_hi))):
                                last = nc.tensor.matmul(bank_of(t)[:, part, 0:cols.stop - cols.start], w[:, (s + u) % 4, kt - a, :],
                                                        x[:, kt, cols], start=kt == 0 and m == 0, stop=kt == FT - 1 and m == 2)
                        if u == 0:
                            turn_out(0, DT - 2) if part == 0 else turn_last(0)
                    last.then_inc(last_part_done, 1)
                turn_last(1)

            def turn_last(part):
                pe.wait_ge(sq_added, DT * 3 - 1)
                pe.wait_ge(sq_ready, DT * 3 + part)
                pe.wait_ge(out_taken, DT - 1)
                for c in LAST_CHUNKS[part]:
                    n = P if c < NC else TS
                    nc.tensor.matmul(X[0:n, 0, c:c + 1], sq_sum[:, CH[c]], ones[:, 0:1], start=True, stop=False)
                    last = nc.tensor.matmul(X[0:n, 0, c:c + 1], sq[:, CH[c]], ones[:, 0:1], start=False, stop=True)
                last.then_inc(final_sums, 1)
                pe.wait_ge(x_gained, DT + part)
                j = DT - 1
                for c in LAST_CHUNKS[part]:
                    out = X[:, 2, CH[c]] if c < NC else X[0:TS, 3, 0:P]
                    last = nc.tensor.transpose(out, x_gain[:, j % 2, CH[c]], ident[:, :])
                last.then_inc(out_turned, 1)

            pe.wait_ge(consts_ready, 2)
            for c, half in X_PIECES:
                if (c, half) == (NC - 1, 0):
                    pe.wait_ge(gains_loaded, 16 * 6)
                    nc.tensor.transpose(X[:, 3, 0:5 * DT], gain_rows[:, :], ident[0:5 * DT, 0:5 * DT]).then_inc(gains_moved, 1)
                pe.wait_ge(x_end_loaded if (c, half) == (NC - 1, 1) else x_loaded[c], 16)
                if c == NC:
                    for j in range(DT):
                        last = nc.tensor.transpose(X[:, 2, j * TS:(j + 1) * TS], x_tok[0:TS, c, j * P:(j + 1) * P],
                                                   ident[0:TS, 0:TS])
                else:
                    if c >= 2:
                        pe.wait_ge(x_taken, X_PIECES.index((c - 2, half)) + 1)
                    for k in range(DT // 2):
                        j = half * DT // 2 + k
                        last = nc.tensor.transpose(dense[c % 2][:, half, k * P:(k + 1) * P], x_tok[:, c, j * P:(j + 1) * P],
                                                   ident[:, :])
                last.then_inc(x_moved, 1)
            for _ in range(KEEP_WARM):
                nc.tensor.transpose(X[:, 1, 0:P], x_tok[:, 0, 0:P], ident[:, :])
            ffn(0, U_F1, T_F1, U_D1, T_D1, 0)

            def p(h, what, cols):
                return proj[:, h % 2, what, cols]

            def step_scores(h):
                if h < H:
                    pe.wait_ge(evicted, T_IN + 4 * h + 3)
                    pe.wait_ge(past_ready, h + 1)
                else:
                    pe.wait_ge(rotated, 2 * (h - H) + 2)
                    pe.wait_ge(evicted, T_IN + 4 * h + 3)
                    pe.wait_ge(normed, h)
                    pe.wait_ge(normed_act, h)
                if h:
                    pe.wait_ge(y_ready, h)
                for c in range(NC):
                    nc.tensor.transpose(X[:, 0, CH[c]], p(h, 1, CH[c]), ident[:, :])
                for c in range(NC):
                    nc.tensor.transpose(X[:, 1, CH[c]], p(h, 2, CH[c]), ident[:, :])
                nc.tensor.transpose(X[0:TS, 2, 0:P], p(h, 1, CH[NC]), ident[:, :])
                nc.tensor.transpose(X[0:TS, 2, P:2 * P], p(h, 2, CH[NC]), ident[:, :])
                for c in range(NC):
                    nc.tensor.matmul(X[:, 3, CH[c]], p(h, 1, CH[c]), p(h, 0, CH[c]), start=True, stop=True)
                nc.tensor.matmul(X[0:TS, 2, 2 * P:2 * P + TS], p(h, 1, CH[NC]), p(h, 0, CH[NC]),
                                 start=True, stop=True).then_inc(scores_done, 1)

            def step_updates(h):
                pe.wait_ge(scores_weighted, h + 1)
                pe.wait_ge(v_ready, h + 1)
                for c in range(NC + 1):
                    n = P if c < NC else TS
                    b, o = (0, c) if c < 3 else (1, c - 3)
                    last = nc.tensor.matmul(X[:, b, o * V1:(o + 1) * V1], k_tail[0:n, c, :], v_tok[0:n, c, :],
                                            start=True, stop=True)
                last.then_inc(updates_done, 1)

            def step_mix(h):
                pe.wait_ge(states_ready, h + 1)
                pe.wait_ge(q_past_ready, h + 1)
                if h == 0:
                    pe.wait_ge(state_loaded, 16 * (2 + H))
                for c in range(NC + 1):
                    n = P if c < NC else TS
                    out = mixed(c, slice(0, V1))
                    last = nc.tensor.matmul(out, scores[0:n, CH[c]], v_tok[0:n, c, :], start=True, stop=c == 0)
                    if c:
                        state = chain[:, c - 1, :] if c < NC else state_in[:, h, :]
                        last = nc.tensor.matmul(out, q_past[:, CH[c]], state, start=False, stop=True)
                last.then_inc(mixed_done, 1)

            def step_turn(h):
                pe.wait_ge(normed, h + 1)
                pe.wait_ge(normed_act, h + 1)
                flat = X[:, 0:2, :].rearrange("p a b -> p (a b)")
                for c in range(NC):
                    nc.tensor.transpose(flat[:, CH[c]], o_tok[:, c, :], ident[:, :])
                nc.tensor.transpose(flat[:, TP:T], o_tok[0:TS, NC, :], ident[0:TS, 0:TS]).then_inc(turned, 1)

            def step_rows(h):
                if h == 0:
                    pe.wait_ge(gate_cols_ready, 1)
                    pe.wait_ge(bm_split_ready, 1)
                else:
                    pe.wait_ge(normed, h)
                    pe.wait_ge(normed_act, h)
                for out, cols in ((X[:, 2, :], slice(0, TP)), (X[:, 3, 0:TS], slice(TP, T))):
                    nc.tensor.matmul(out, sel_r[:, h, :], bm_split[:, 0, cols], start=True, stop=False)
                    last = nc.tensor.matmul(out, sel_r[:, h, :], bm_split[:, 1, cols], start=False, stop=True)
                last.then_inc(rows_spread, 1)

            def gate_columns():
                pe.wait_ge(gate_rows_ready, 1)
                for c in range(NC):
                    nc.tensor.transpose(X[:, 2, c * 64:(c + 1) * 64], row_cols[:, CH[c]], ident[0:64, 0:64])
                nc.tensor.transpose(X[0:TS, 2, NC * 64:(NC + 1) * 64], row_cols[:, TP:T], ident[0:64, 0:64])
                for h in range(H):
                    last = nc.tensor.matmul(X[:, 3, h * (NC + 1):(h + 1) * (NC + 1)], sel[:, h, :],
                                            row_small[:, M_PREV:M_PREV + NC + 1], start=True, stop=True)
                last.then_inc(gate_cols_moved, 1)

            pe.wait_ge(w_lo_ready, U_GATE + 1)
            tile_free(T_GATE)
            product(U_GATE, bank_of(T_GATE), *xg, range(SUMS_K[1]), True, False, ready=xg_ready(1))
            norm_sums_of(1)
            product(U_GATE, bank_of(T_GATE), *xg, range(SUMS_K[1], DT), False, True, ready=xg_ready(1)).then_inc(unit_done, 1)
            for h in range(2 * H):
                for u in range(4):
                    s, t = U_IN + 4 * h + u, T_IN + 4 * h + u
                    pe.wait_ge(w_lo_ready, s + 1)
                    tile_free(t)
                    if h == 0 and u == 2:
                        product(s, bank_of(t), *xg, range(2), True, False)
                        gate_columns()
                        product(s, bank_of(t), *xg, range(2, DT), False, True).then_inc(unit_done, 1)
                    elif u == 3:
                        product(s, bank_of(t), *xg, range(1), True, False)
                        if h:
                            step_turn(h - 1)
                        if h < H:
                            step_rows(h)
                        product(s, bank_of(t), *xg, range(1, DT), False, True).then_inc(unit_done, 1)
                    else:
                        product(s, bank_of(t), *xg, range(DT), True, True).then_inc(unit_done, 1)
                    if u == 3:
                        step_scores(h)
                    elif h and u < 2:
                        (step_updates, step_mix)[u](h - 1)
            for j, part, step in ((0, range(0, 4), step_updates), (0, range(4, DT - 1), step_mix), (1, range(0, DT - 1), None),
                                  (2, range(0, 2), step_turn), (2, range(2, DT - 1), None)):
                if part[0] == 0:
                    pe.wait_ge(w_lo_ready, U_OUT + j + 1)
                    if j < 2:
                        tile_free(T_OUT + j)
                    else:
                        pe.wait_ge(normed, 2 * H)
                        pe.wait_ge(normed_act, 2 * H)
                if j == 0:
                    pe.wait_ge(y_lo_ready, part[-1] + 1)
                product(U_OUT + j, out_tile(j), y_hi, y_lo, part, part[0] == 0, False)
                if step:
                    step(2 * H - 1)
            pe.wait_ge(y_lo_ready, 2 * H)
            for j in range(3):
                product(U_OUT + j, out_tile(j), y_hi, y_lo, [DT - 1], False, True).then_inc(unit_done, 1)
            for j in range(3, DT):
                pe.wait_ge(w_lo_ready, U_OUT + j + 1)
                if j < 5:
                    pe.wait_ge(evicted, T_OUT + j - 2)
                else:
                    tile_free(T_OUT + j)
                product(U_OUT + j, out_tile(j), y_hi, y_lo, range(DT), True, True).then_inc(unit_done, 1)

            ffn(1, U_F2, T_F2, U_D2, T_D2, 2)

        @block.scalar
        def _(act):
            link = chained(act, act_step)


            def split_hi(i, s, step):
                if s >= U_END:
                    return
                if s == U_GATE:
                    act.wait_ge(gates_loaded, 16 * 4)
                    act.wait_ge(gate_slots_zeroed, 2)
                    for n in range(2):
                        last = nc.scalar.activation(w_hi[:, s % 4, :, 32 * n:32 * n + H], w_gates[:, :, H * n:H * (n + 1)], ACT.Copy)
                    last.then_inc(w_hi_ready, 1)
                    return
                loads = len([m for m in range(s % RAW, s + 1, RAW) if m != U_GATE])
                act.wait_ge(w_loaded[s % RAW], 16 * loads + 16 // RAW * step * i)
                source = w_raw[:, s % RAW, 0:k_tiles(s), :]
                if s >= 4:
                    act.wait_ge(unit_done, s - 3 + step * i)
                nc.scalar.activation(w_hi[:, s % 4, 0:k_tiles(s), :], source, ACT.Copy).then_inc(w_hi_ready, 1)

            def square(j, norm):
                act.wait_ge(sq_added, DT * (norm - 1) + j)
                nc.scalar.activation(sq[:, :], xT[:, j, :], ACT.Square).then_inc(sq_ready, 1)

            def normed_hi(i, j, t, g, step):
                if t is not None:
                    act.wait_ge(evicted, t + 1 + step * i)
                act.wait_ge(gains_ready, 1)
                nc.scalar.activation(xg_hi[:, j + step * i, :], xT[:, j + step * i, :], ACT.Copy,
                                     scale=gains[:, bass.ds(g + j + step * i, 1)]).then_inc(xg_hi_ready, 1)

            def root(n):
                act.wait_ge(norm_sums, n + 1)
                nc.scalar.activation(rstd[:, :].rearrange("p (a b) -> p a b", a=2), X[:, 0:2, 0:TH], ACT.Sqrt, scale=1.0 / D,
                                     bias=eps[:, :]).then_inc(norm_root, 1)

            def ffn(n, u_base, t_base, d_base, td_base, norm):
                def gate_up(i, s, g):
                    for u in range(4):
                        split_hi(i, s + u + 2, 4)
                        t = t_base + s - u_base + u
                        j = 2 * g + u // 2
                        if g == 0 and u == 0:
                            root(norm)
                        act.wait_ge(evicted, t + 1 + 4 * i)
                        if u % 2 == 0:
                            if n or j:
                                act.wait_ge(silu_scaled, FT * n + j + 2 * i)
                            nc.scalar.activation(gate_s[:, :], gate_n[:, :], ACT.Silu).then_inc(silu_ready, 1)
                        else:
                            act.wait_ge(gains_ready, 1)
                            nc.scalar.activation(h_hi[:, j + 2 * i, :], h_f[:, :], ACT.Copy).then_inc(h_hi_ready, 1)

                groups(act, u_base, 2 * FT, 4, gate_up)

                def down(i, s, g):
                    for v in range(2):
                        for u in range(4):
                            split_hi(i, s + 4 * v + u + 2, 8)
                        j = 2 * g + v
                        if n and j == DT - 1:
                            for part in range(2):
                                last_part(part)
                            return
                        if n == 0:
                            normed_hi(i, j, td_base + j, G_MIX, 2)
                        else:
                            act.wait_ge(evicted, td_base + j + 1 + 2 * i)
                            if j >= 2:
                                act.wait_ge(out_turned, j - 1 + 2 * i)
                            act.wait_ge(gains_ready, 1)
                            nc.scalar.activation(x_gain[:, j % 2, :], xT[:, j + 2 * i, :], ACT.Copy,
                                                 scale=gains[:, bass.ds(G_FINAL + j + 2 * i, 1)]).then_inc(x_gained, 1)

                groups(act, d_base, 4 * DT, 8, down)

            def last_part(part):
                cols, chunks = LAST_COLS[part], LAST_CHUNKS[part]
                act.wait_ge(last_part_taken, part + 1)
                act.wait_ge(out_turned, DT - 2)
                nc.scalar.activation(x_gain[:, (DT - 1) % 2, cols], xT[:, DT - 1, cols], ACT.Copy,
                                     scale=gains[:, G_FINAL + DT - 1:G_FINAL + DT]).then_inc(x_gained, 1)
                act.wait_ge(final_sums, part + 1)
                a = chunks[0]
                last = nc.scalar.activation(rms_tok[:, 0, a:a + 2], X[:, 0, a:a + 2], ACT.Sqrt, scale=1.0 / D, bias=eps[:, :])
                if NC in chunks:
                    last = nc.scalar.activation(rms_tok[0:TS, 0, NC:NC + 1], X[0:TS, 0, NC:NC + 1], ACT.Sqrt, scale=1.0 / D,
                                                bias=eps[0:TS, :])
                last.then_inc(final_root, 1)
                act.wait_ge(final_rstd, part + 1)
                act.wait_ge(out_taken, DT + part)
                c = chunks[1]
                nc.scalar.activation(y_tok[:, c, :], y_tok[:, c, :], ACT.Copy, scale=rms_tok[:, 1, c:c + 1])\
                    .then_inc(y_done[c], 1)

            act.wait_ge(consts_ready, 2)
            link(nc.scalar.activation(unused[:, :], eps[:, :], ACT.Square))
            for n, c in enumerate(X_ORDER):
                act.wait_ge(x_loaded[c], 16)
                if c == NC - 1:
                    act.wait_ge(x_end_loaded, 16)
                if n:
                    act.wait_ge(x_summed, n)
                r = P if c < NC else TS
                nc.scalar.activation(x_squared[0:r, :], x_tok[0:r, c, :], ACT.Square, accum_out=x_sums[0:r, c:c + 1])\
                    .then_inc(x_summed, 1)
                if c == 2:
                    split_hi(0, 0, 0)
            act.wait_ge(gains_moved, 1)
            nc.scalar.activation(gains[:, :], X[:, 3, 0:5 * DT], ACT.Copy).then_inc(gains_ready, 1)
            for j in range(DT):
                act.wait_ge(x_taken, len(X_PIECES) - (j < DT // 2))
                normed_hi(0, j, None, G_FFN1, 0)
            split_hi(0, 1, 0)

            ffn(0, U_F1, T_F1, U_D1, T_D1, 0)

            def step_values(h):
                act.wait_ge(scores_done, h + 1)
                if h:
                    act.wait_ge(mixed_done, h)
                if h == 0:
                    act.wait_ge(mixer_consts, 1)
                if h == H:
                    act.wait_ge(table_loaded, 16)
                if h >= H:
                    nc.scalar.activation(k_tail[:, 0:NC, :], X[:, 0, :].rearrange("p (c d) -> p c d", c=NC), ACT.Copy,
                                         scale=table[:, TAIL + h - H:TAIL + h - H + 1])
                nc.scalar.activation(v_tok[:, 0:NC, 0:P], X[:, 1, :].rearrange("p (c d) -> p c d", c=NC), ACT.Copy)\
                    .then_inc(v_ready, 1)

            def step_gate(h):
                act.wait_ge(evicted, T_IN + 4 * h + 4)
                if h:
                    act.wait_ge(y_ready, h)
                nc.scalar.activation(gate_act[:, :], proj[:, h % 2, 3, :], ACT.Sigmoid if h < H else ACT.Silu)\
                    .then_inc(gate_act_ready, 1)

            def step_o(h):
                act.wait_ge(shift_ready, h + 1)
                if h:
                    act.wait_ge(turned, h)
                for c in ACT_CHUNKS:
                    n = P if c < NC else TS
                    last = nc.scalar.activation(o_tok[0:n, c, :], mixed(c), ACT.Identity,
                                                scale=small[0:n, 4, c:c + 1], bias=small[0:n, 5, c:c + 1])
                last.then_inc(normed_act, 1)

            def step_y(h):
                act.wait_ge(y_ready, h + 1)
                nc.scalar.activation(y_hi(h), y_f[:, :], ACT.Copy).then_inc(y_hi_ready, 1)

            def step_weights(h):
                act.wait_ge(arg_ready, h + 1)
                if h:
                    act.wait_ge(scores_weighted, h)
                for c in range(NC + 1):
                    n = P if c < NC else TS
                    last = nc.scalar.activation(weights[0:n, CH[c]], weights_arg[0:n, CH[c]], ACT.Exp,
                                                bias=key_col[0:n, c, h:h + 1])
                last.then_inc(weights_ready, 1)
                if h:
                    act.wait_ge(q_past_ready, h)
                    act.wait_ge(states_ready, h)
                for c in range(NC + 1):
                    source = X[:, 2, CH[c]] if c < NC else X[:, 3, 0:TS]
                    last = nc.scalar.activation(past[:, CH[c]], source, ACT.Exp, bias=m_prev_all[:, h, c:c + 1])
                last.then_inc(past_ready, 1)

            split_hi(0, U_IN + 1, 0)
            root(1)
            split_hi(0, U_IN + 2, 0)
            link(nc.scalar.activation(unused[:, :], eps[:, :], ACT.Exp))
            act.wait_ge(gates_biased, 1)
            link(nc.scalar.activation(rows[:, E_ROW, :], rows[:, F_ROW, :], ACT.Abs))
            link(nc.scalar.activation(rows[:, LF_ROW, :], rows[:, E_ROW, :], ACT.Exp, scale=-1.0))
            nc.scalar.activation(rows[:, E_ROW, :], rows[:, LF_ROW, :], ACT.Ln, bias=ones[0:H, 0:1]).then_inc(gates_ln, 1)
            link(nc.scalar.activation(unused[:, :], eps[:, :], ACT.Exp))
            for h in range(2 * H):
                for u in range(4):
                    if h or u:
                        split_hi(0, U_IN + 4 * h + u + 2, 0)
                    if h and u == 0:
                        step_gate(h - 1)
                    if h and u == 1:
                        step_o(h - 1)
                    if h == 0 and u == 2:
                        act.wait_ge(gate_rows_ready, 1)
                        nc.scalar.activation(bm_split[:, 0, :], rows[:, BM_ROW, :], ACT.Copy).then_inc(bm_hi_ready, 1)
                        act.wait_ge(mixer_consts, 1)
                        nc.scalar.activation(sel_r[:, :, :], sel[:, :, :], ACT.Copy)
                        act.wait_ge(gate_cols_moved, 1)
                        cols = X[:, 2, 0:(NC + 1) * 64].rearrange("p (c q) -> p c q", q=64)
                        nc.scalar.activation(key_col[:, 0:NC, :], cols[:, 0:NC, 0:H], ACT.Copy)
                        nc.scalar.activation(key_col[0:TS, NC, :], cols[0:TS, NC, 0:H], ACT.Copy)
                        nc.scalar.activation(neg_m_exp[:, 0:NC, :], cols[:, 0:NC, 32:32 + H], ACT.Exp)
                        nc.scalar.activation(neg_m_exp[0:TS, NC, :], cols[0:TS, NC, 32:32 + H], ACT.Exp)
                        nc.scalar.activation(m_prev_all[:, :, :], X[:, 3, 0:H * (NC + 1)].rearrange("p (h c) -> p h c", h=H),
                                             ACT.Copy).then_inc(gate_cols_ready, 1)
                        act.wait_ge(gate_cols_ready, 1)
                    if u == 2 and h < H:
                        step_weights(h)
                    if u == 2 and h:
                        step_y(h - 1)
                    if u == 3:
                        step_values(h)
            step_gate(2 * H - 1)
            split_hi(0, U_OUT + 2, 0)
            step_o(2 * H - 1)
            split_hi(0, U_OUT + 3, 0)
            step_y(2 * H - 1)
            for j in range(DT):
                if j > 1:
                    split_hi(0, U_OUT + j + 2, 0)
                normed_hi(0, j, T_OUT + j, G_FFN2, 0)
                square(j, 2)

            ffn(1, U_F2, T_F2, U_D2, T_D2, 2)

        @block.vector
        def _(dve):
            link = chained(dve, dve_step)

            def split_lo(i, s, step):
                if s >= U_END:
                    return
                dve.wait_ge(w_hi_ready, s + 1 + step * i)
                if s == U_GATE:
                    for n in range(2):
                        last = nc.vector.tensor_tensor(w_lo[:, s % 4, :, 32 * n:32 * n + H], w_gates[:, :, H * n:H * (n + 1)],
                                                       w_hi[:, s % 4, :, 32 * n:32 * n + H].bitcast(F32), ALU.subtract)
                    last.then_inc(w_lo_ready, 1)
                    return
                nk = k_tiles(s)
                nc.vector.tensor_tensor(w_lo[:, s % 4, 0:nk, :], w_raw[:, s % RAW, 0:nk, :],
                                        w_hi[:, s % 4, 0:nk, :].bitcast(F32), ALU.subtract).then_inc(w_lo_ready, 1)

            def normed_lo(i, j, norm, g, step):
                dve.wait_ge(xg_hi_ready, DT * norm + j + 1 + step * i)
                nc.vector.scalar_tensor_tensor(
                    xg_lo[:, j + step * i, :], xT[:, j + step * i, :], gains[:, bass.ds(g + j + step * i, 1)],
                    xg_hi[:, j + step * i, :].bitcast(F32), ALU.mult, ALU.subtract).then_inc(xg_lo_ready, 1)

            def invert_root(n):
                dve.wait_ge(norm_root, n + 1)
                nc.vector.reciprocal(rstd[:, :], rstd[:, :]).then_inc(rstd_ready, 1)
                dve.wait_ge(rstd_ready, n + 1)

            def take_out(i, j):
                dve.wait_ge(out_turned, j + 1 + 2 * i)
                b = 2 * (j % 2)
                cols = bass.ds((j + 2 * i) * P, P)
                nc.vector.tensor_copy(y_tok[:, 0:NC, cols], X[:, b, :].rearrange("p (c d) -> p c d", c=NC))
                nc.vector.tensor_copy(y_tok[0:TS, NC, cols], X[0:TS, b + 1, 0:P]).then_inc(out_taken, 1)

            def ffn(n, u_base, t_base, d_base, td_base, norm):
                def gate_up(i, s, g):
                    for u in range(4):
                        split_lo(i, s + u + 2, 4)
                        t = t_base + s - u_base + u
                        j = 2 * g + u // 2
                        if g == 0 and u == 0:
                            invert_root(norm)
                        dve.wait_ge(unit_done, s + u + 1 + 4 * i)
                        if u % 2 == 0:
                            if n or j:
                                dve.wait_ge(silu_ready, FT * n + j + 2 * i)
                            nc.vector.tensor_tensor(split_cols(gate_n[:, :]), halves(bank_of(t)), split_cols(rstd[:, :]),
                                                    ALU.mult).then_inc(evicted, 1)
                        else:
                            dve.wait_ge(silu_scaled, FT * n + j + 1 + 2 * i)
                            if n or j:
                                dve.wait_ge(h_lo_ready, FT * n + j + 2 * i)
                            nc.vector.tensor_tensor(split_cols(h_f[:, :]), halves(bank_of(t)), split_cols(gate_r[:, :]),
                                                    ALU.mult).then_inc(evicted, 1)

                groups(dve, u_base, 2 * FT, 4, gate_up)

                def down(i, s, g):
                    for v in range(2):
                        for u in range(4):
                            split_lo(i, s + 4 * v + u + 2, 8)
                        j = 2 * g + v
                        if n and j == DT - 1:
                            for part in range(2):
                                last_part(part, bank_of(td_base + j))
                            return
                        add_residual(s + 4 * v + 3, 8, i, j, bank_of(td_base + j), 0.5, 2)
                        dve.wait_ge(evicted, td_base + j + 1 + 2 * i)
                        if norm or j:
                            dve.wait_ge(sq_added, DT * norm + j + 2 * i)
                        nc.vector.tensor_tensor(sq[:, :], xT[:, j + 2 * i, :], xT[:, j + 2 * i, :], ALU.mult).then_inc(sq_ready, 1)
                        if n == 0:
                            normed_lo(i, j, 1, G_MIX, 2)
                        elif not (g == 0 and v == 0):
                            take_out(i, j - 1)

                groups(dve, d_base, 4 * DT, 8, down)

            def add_residual(s, unit_step, i, j, tile, factor, step):
                dve.wait_ge(unit_done, s + 1 + unit_step * i)
                x = split_cols(xT[:, j + step * i, :])
                nc.vector.scalar_tensor_tensor(x, halves(tile), factor, x, ALU.mult, ALU.add).then_inc(evicted, 1)

            def last_part(part, tile):
                cols, chunks, j = LAST_COLS[part], LAST_CHUNKS[part], DT - 1
                dve.wait_ge(last_part_done, part + 1)
                nc.vector.scalar_tensor_tensor(xT[:, j, cols], tile[:, part, 0:cols.stop - cols.start], 0.5, xT[:, j, cols],
                                               ALU.mult, ALU.add).then_inc(last_part_taken, 1)
                dve.wait_ge(last_part_taken, part + 1)
                dve.wait_ge(sq_added, DT * 3 - 1)
                nc.vector.tensor_tensor(sq[:, cols], xT[:, j, cols], xT[:, j, cols], ALU.mult).then_inc(sq_ready, 1)
                if part == 0:
                    take_out(0, j - 1)
                dve.wait_ge(out_turned, j + 1 + part)
                a = chunks[0]
                last = nc.vector.tensor_copy(y_tok[:, a:a + 2, j * P:(j + 1) * P],
                                             X[:, 2, a * P:(a + 2) * P].rearrange("p (c d) -> p c d", c=2))
                if NC in chunks:
                    last = nc.vector.tensor_copy(y_tok[0:TS, NC, j * P:(j + 1) * P], X[0:TS, 3, 0:P])
                last.then_inc(out_taken, 1)
                dve.wait_ge(final_root, part + 1)
                last = nc.vector.reciprocal(rms_tok[:, 1, a:a + 2], rms_tok[:, 0, a:a + 2])
                if NC in chunks:
                    last = nc.vector.reciprocal(rms_tok[0:TS, 1, NC:NC + 1], rms_tok[0:TS, 0, NC:NC + 1])
                last.then_inc(final_rstd, 1)
                dve.wait_ge(final_rstd, part + 1)
                dve.wait_ge(out_taken, DT + part)
                for c in (a, NC) if NC in chunks else (a,):
                    n = P if c < NC else TS
                    nc.vector.tensor_scalar(y_tok[0:n, c, :], y_tok[0:n, c, :], rms_tok[0:n, 1, c:c + 1], None, ALU.mult)\
                        .then_inc(y_done[c], 1)

            for n, (c, half) in enumerate(X_PIECES):
                dve.wait_ge(x_moved, n + 1)
                if c < NC:
                    tiles = dense[c % 2][:, half, :].rearrange("p (k d) -> p k d", d=P)
                    a = half * DT // 2
                    nc.vector.tensor_copy(xT[:, a:a + DT // 2, CH[c]], tiles).then_inc(x_taken, 1)
                else:
                    tiles = X[:, 2, 0:DT * TS].rearrange("p (k d) -> p k d", d=TS)
                    nc.vector.tensor_copy(xT[:, :, CH[c]], tiles).then_inc(x_taken, 1)
            for j in range(DT):
                normed_lo(0, j, 0, G_FFN1, 0)
            dve.wait_ge(w_lo_ready, 1)
            split_lo(0, 1, 0)

            ffn(0, U_F1, T_F1, U_D1, T_D1, 0)

            def take(t, out, scale=None):
                if scale is None:
                    return nc.vector.tensor_tensor(split_cols(out), halves(bank_of(t)), split_cols(rstd[:, :]), ALU.mult)
                return nc.vector.scalar_tensor_tensor(split_cols(out), halves(bank_of(t)), scale, split_cols(rstd[:, :]),
                                                      ALU.mult, ALU.mult)

            def take_rotated(t, n):
                if n:
                    dve.wait_ge(rotated, n)
                else:
                    dve.wait_ge(tables_scaled, 1)
                tile = halves(bank_of(t))
                nc.vector.tensor_tensor(split_cols(rot[:, 0, :]), tile, split_cols(table[:, COS:COS + T]), ALU.mult)
                for a, b in ((0, 64), (64, 0)):
                    last = nc.vector.tensor_tensor(split_cols(rot[a:a + 64, 1, :]), tile[b:b + 64],
                                                   split_cols(table[b:b + 64, SIN:SIN + T]), ALU.mult)
                last.then_inc(evicted, 1)

            def gate_rows_start():
                dve.wait_ge(unit_done, U_GATE + 1)
                tile = halves(bank_of(T_GATE))
                nc.vector.tensor_tensor(split_cols(rows[:, I_ROW, :]), tile[0:H], split_cols(rstd[0:H, :]), ALU.mult)
                nc.vector.tensor_tensor(split_cols(rows[:, F_ROW, :]), tile[32:32 + H], split_cols(rstd[32:32 + H, :]), ALU.mult)\
                    .then_inc(evicted, 1)
                dve.wait_ge(evicted, T_GATE + 1)
                dve.wait_ge(gates_loaded, 16 * 4)
                nc.vector.tensor_scalar(rows[:, I_ROW, :], rows[:, I_ROW, :], row_small[:, 0:1], None, ALU.add)
                nc.vector.tensor_scalar(rows[:, F_ROW, :], rows[:, F_ROW, :], row_small[:, 1:2], None, ALU.add)\
                    .then_inc(gates_biased, 1)
                nc.vector.tensor_scalar(row_small[:, M_PREV:M_PREV + 1], row_small[:, 2:3], 0.0, None, ALU.mult)
                nc.vector.tensor_copy(row_small[:, M_PREV + NC:M_PREV + NC + 1], row_small[:, 2:3])

            def gate_rows_end():
                dve.wait_ge(gates_ln, 1)
                r = lambda n, cols=slice(0, T): rows[:, n, cols]
                link(nc.vector.scalar_tensor_tensor(r(LF_ROW), r(F_ROW), 0.0, r(E_ROW), ALU.min, ALU.subtract))
                nc.vector.tensor_tensor_scan(r(M_ROW, slice(0, TP)), r(LF_ROW, slice(0, TP)), r(I_ROW, slice(0, TP)), 0.0,
                                             ALU.add, ALU.max)
                nc.vector.tensor_tensor_scan(r(M_ROW, CH[NC]), r(LF_ROW, CH[NC]), r(I_ROW, CH[NC]), row_small[:, 2:3],
                                             ALU.add, ALU.max)
                for c in range(NC + 1):
                    n = P if c < NC else TS
                    last = nc.vector.tensor_tensor_scan(r(B_ROW, CH[c]), ones[0:H, 0:n], r(LF_ROW, CH[c]), 0.0, ALU.mult, ALU.add)
                link(last)
                dve.wait_ge(mixer_consts, 1)
                nc.vector.tensor_tensor(r(BM_ROW), r(B_ROW), r(M_ROW), ALU.subtract)
                nc.vector.tensor_tensor(row_cols[0:H, :], r(I_ROW), r(B_ROW), ALU.subtract)
                nc.vector.tensor_scalar(row_cols[32:32 + H, :], r(M_ROW), -1.0, None, ALU.mult)
                nc.vector.tensor_copy(row_small[:, M_PREV + 1:M_PREV + NC], rows[:, M_ROW, P - 1:TP - 1:P])\
                    .then_inc(gate_rows_ready, 1)
                nc.vector.tensor_copy(row_small[:, M_OUT:M_OUT + 1], rows[:, M_ROW, TP - 1:TP])
                nc.vector.tensor_copy(row_small[:, M_OUT + 1:M_OUT + 2], rows[:, M_ROW, T - 1:T])

            def step_scores(h):
                dve.wait_ge(scores_done, h + 1)
                if h:
                    dve.wait_ge(mixed_done, h)
                grid = lambda ap: ap.rearrange("p (c d) -> p c d", c=NC)
                if h < H:
                    dve.wait_ge(weights_ready, h + 1)
                    nc.vector.tensor_tensor(scores[:, 0:TP], X[:, 3, :], weights[:, 0:TP], ALU.mult)
                    nc.vector.tensor_tensor(scores[0:TS, TP:T], X[0:TS, 2, 2 * P:2 * P + TS], weights[0:TS, TP:T], ALU.mult)
                    keep = grid(weights[:, 0:TP])[:, :, P - 1:P].broadcast_to([P, NC, P])
                    nc.vector.tensor_tensor(k_tail[:, 0:NC, :], grid(X[:, 0, :]), keep, ALU.mult)
                    nc.vector.tensor_scalar(k_tail[0:TS, NC, :], X[0:TS, 2, 0:P], weights[0:TS, T - 1:T], None, ALU.mult)
                else:
                    d = DECAY + (h - H) * P
                    decay = table[:, d:d + P].rearrange("p (c d) -> p c d", c=1)
                    nc.vector.tensor_tensor(grid(scores[:, 0:TP]), grid(X[:, 3, :]), decay.broadcast_to([P, NC, P]), ALU.mult)
                    nc.vector.tensor_tensor(scores[0:TS, TP:T], X[0:TS, 2, 2 * P:2 * P + TS], table[0:TS, d:d + TS], ALU.mult)
                    nc.vector.tensor_scalar(k_tail[0:TS, NC, :], X[0:TS, 2, 0:P],
                                            table[0:TS, TAIL_S + h - H:TAIL_S + h - H + 1], None, ALU.mult)
                nc.vector.tensor_copy(v_tok[0:TS, NC, 0:P], X[0:TS, 2, P:2 * P]).then_inc(scores_weighted, 1)

            def step_states(h):
                dve.wait_ge(updates_done, h + 1)
                if h == 0:
                    dve.wait_ge(state_loaded, 16 * (2 + H))
                add = lambda c: X[:, 0 if c < 3 else 1, (c % 3) * V1:(c % 3 + 1) * V1]

                def kept(c, n):
                    if h < H:
                        return past[:, CH[c].stop - 1:CH[c].stop]
                    return float(np.exp(LOG_GAMMA[h - H] * np.float32(n)))

                sample_in = state_in[:, h, :]
                nc.vector.scalar_tensor_tensor(state_s[:, h, :], sample_in, kept(NC, TS), X[:, 1, V1:2 * V1], ALU.mult, ALU.add)
                link(nc.vector.tensor_copy(chain[:, 0, :], add(0)))
                for c in range(1, NC):
                    out = chain[:, c, :] if c < NC - 1 else state_p[:, h, :]
                    last = nc.vector.scalar_tensor_tensor(out, chain[:, c - 1, :], kept(c, P), add(c), ALU.mult, ALU.add)
                    if c < NC - 1:
                        link(last)
                last.then_inc(states_ready, 1)

            def step_norm(h):
                dve.wait_ge(mixed_done, h + 1)
                den, inv, var, root, scale, shift = (small[:, k, :] for k in range(6))
                if h < H:
                    parts = []
                    for a, b, n in ((0, 3, P), (3, 4, P), (4, 5, TS)):
                        total = X[0:n, 2 + a // 3, (a % 3) * V1:(a % 3 + b - a) * V1].rearrange("p (c d) -> p c d", d=V1)[:, :, P]
                        parts.append((den[0:n, a:b], total, neg_m_exp[0:n, a:b, h]))
                    for out, total, floor in parts:
                        nc.vector.scalar_tensor_tensor(out, total, -1.0, floor, ALU.mult, ALU.max)
                for c in range(NC + 1):
                    last = nc.vector.bn_stats(stats[0:P if c < NC else TS, c, :], mixed(c))
                link(last)
                if h < H:
                    for out, total, _ in parts:
                        nc.vector.tensor_tensor(out, total, out, ALU.max)
                for c in range(NC + 1):
                    n = P if c < NC else TS
                    last = nc.vector.bn_aggr(mean_var[0:n, c, :], stats[0:n, c, :])
                link(last)
                if h < H:
                    link(nc.vector.reciprocal(inv, den))
                    link(nc.vector.tensor_tensor(var, mean_var[:, :, 1], inv, ALU.mult))
                    link(nc.vector.tensor_tensor(var, var, inv, ALU.mult))
                    nc.vector.tensor_scalar(var, var, GN_EPS, None, ALU.add).then_inc(var_ready, 1)
                    dve.wait_ge(root_ready, h + 1)
                    link(nc.vector.tensor_tensor(scale, root, inv, ALU.mult))
                else:
                    nc.vector.tensor_scalar(var, mean_var[:, :, 1], GN_EPS, None, ALU.add).then_inc(var_ready, 1)
                    dve.wait_ge(root_ready, h + 1)
                    link(nc.vector.tensor_copy(scale, root))
                nc.vector.scalar_tensor_tensor(shift, mean_var[:, :, 0], -1.0, scale, ALU.mult, ALU.mult).then_inc(shift_ready, 1)
                dve.wait_ge(shift_ready, h + 1)
                for c in range(ACT_CHUNKS[0]):
                    last = nc.vector.tensor_scalar(o_tok[:, c, :], mixed(c), scale[:, c:c + 1], shift[:, c:c + 1],
                                                   ALU.mult, ALU.add)
                last.then_inc(normed, 1)

            def step_y(h):
                dve.wait_ge(turned, h + 1)
                dve.wait_ge(gate_act_ready, h + 1)
                if h:
                    dve.wait_ge(y_lo_ready, h)
                flat = X[:, 0:2, :].rearrange("p a b -> p (a b)")
                nc.vector.scalar_tensor_tensor(y_f[:, :], flat[:, 0:T], gains[:, G_GN + h:G_GN + h + 1], gate_act[:, :],
                                               ALU.mult, ALU.mult).then_inc(y_ready, 1)

            def step_arg(h):
                dve.wait_ge(rows_spread, h + 1)
                if h:
                    dve.wait_ge(weights_ready, h)
                grid = lambda ap: ap.rearrange("p (c d) -> p c d", c=NC)
                m = mask[:, :].rearrange("p (c d) -> p c d", c=1).broadcast_to([P, NC, P])
                nc.vector.tensor_tensor(grid(weights_arg[:, 0:TP]), grid(X[:, 2, :]), m, ALU.add)
                nc.vector.tensor_tensor(weights_arg[0:TS, TP:T], X[0:TS, 3, 0:TS], mask[0:TS, 0:TS], ALU.add).then_inc(arg_ready, 1)

            split_lo(0, U_IN + 1, 0)
            invert_root(1)
            gate_rows_start()
            for h in range(2 * H):
                for u in range(4):
                    s, t = U_IN + 4 * h + u, T_IN + 4 * h + u
                    split_lo(0, s + 2, 0)
                    dve.wait_ge(unit_done, s + 1)
                    if h >= 2:
                        dve.wait_ge(gate_act_ready, h - 1)
                        dve.wait_ge(scores_done, h - 1)
                        dve.wait_ge(q_past_ready, h - 1)
                    if h >= H and u == 0:
                        step_states(h - 1)
                    if h >= H and u < 2:
                        take_rotated(t, 2 * (h - H) + u)
                    else:
                        take(t, proj[:, h % 2, u, :], P ** -0.5 if u == 1 else None).then_inc(evicted, 1)
                    if h == 0 and u == 0:
                        gate_rows_end()
                    if h == 0 and u == 1:
                        dve.wait_ge(bm_hi_ready, 1)
                        nc.vector.tensor_tensor(bm_split[:, 1, :], rows[:, BM_ROW, :], bm_split[:, 0, :].bitcast(F32),
                                                ALU.subtract).then_inc(bm_split_ready, 1)
                    if u == 3:
                        step_scores(h)
                    if u == 2 and h < H:
                        step_arg(h)
                    if h and u < 3 and not (h >= H and u == 0):
                        (step_states, step_norm, step_y)[u](h - 1)
            step_states(2 * H - 1)
            split_lo(0, U_OUT + 2, 0)
            step_norm(2 * H - 1)
            step_y(2 * H - 1)
            dve.wait_ge(y_hi_ready, 2 * H)
            nc.vector.tensor_tensor(y_lo(2 * H - 1), y_f[:, :], y_hi(2 * H - 1).bitcast(F32), ALU.subtract).then_inc(y_lo_ready, 1)
            split_lo(0, U_OUT + 3, 0)
            for j in range(3):
                add_residual(U_OUT + j, 0, 0, j, out_tile(j), 1.0, 0)
            for j in range(DT):
                if j > 1:
                    split_lo(0, U_OUT + j + 2, 0)
                if j > 2:
                    add_residual(U_OUT + j, 0, 0, j, out_tile(j), 1.0, 0)
                normed_lo(0, j, 2, G_FFN2, 0)

            ffn(1, U_F2, T_F2, U_D2, T_D2, 2)

        @block.gpsimd
        def _(pool):
            link = chained(pool, pool_step)

            def triangle(ap, pattern, op, fill, base=0, mult=1):
                return nc.gpsimd.affine_select(out=ap, in_=ap, compare_op=op, fill=fill, base=base, pattern=pattern,
                                               channel_multiplier=mult)

            link(nc.gpsimd.memset(ident[:, :], 0.0))
            link(triangle(ident[:, :], [[-1, P]], ALU.not_equal, 1.0))
            nc.gpsimd.memset(ones[:, :], 1.0).then_inc(consts_ready, 1)
            nc.gpsimd.memset(eps[:, :], EPS).then_inc(consts_ready, 1)

            def add_square(i, j, norm, step, reset=False):
                if reset:
                    pool.wait_ge(norm_sums, norm)
                    link(nc.gpsimd.memset(sq_sum[:, :], 0.0))
                pool.wait_ge(sq_ready, DT * (norm - 1) + j + 1 + step * i)
                if not reset:
                    pool.wait_ge(sq_added, DT * (norm - 1) + j + step * i)
                nc.gpsimd.tensor_tensor(sq_sum[:, :], sq_sum[:, :], sq[:, :], ALU.add).then_inc(sq_added, 1)

            def ffn(n, u_base, norm):
                def gate_up(i, s, g):
                    for v in range(2):
                        j = 2 * g + v
                        if g == 0 and v == 0:
                            pool.wait_ge(rstd_ready, norm + 1)
                        pool.wait_ge(silu_ready, FT * n + j + 1 + 2 * i)
                        nc.gpsimd.tensor_tensor(gate_r[:, :], gate_s[:, :], rstd[:, :], ALU.mult).then_inc(silu_scaled, 1)
                        pool.wait_ge(h_hi_ready, FT * n + j + 1 + 2 * i)
                        nc.gpsimd.tensor_tensor(h_lo[:, j + 2 * i, :], h_f[:, :], h_hi[:, j + 2 * i, :].bitcast(F32),
                                                ALU.subtract).then_inc(h_lo_ready, 1)

                groups(pool, u_base, 2 * FT, 4, gate_up)

                def down(i, s, g):
                    for v in range(2):
                        if n and 2 * g + v == DT - 1:
                            return
                        add_square(i, 2 * g + v, norm + 1, 2, reset=g == 0 and v == 0)
                        if n == 0 and g == DT // 2 - 1 and v == 0:
                            pool.wait_ge(unit_done, U_GATE - 3)
                            nc.gpsimd.memset(w_hi[:, U_GATE % 4, :, :].bitcast(F32), 0.0).then_inc(gate_slots_zeroed, 1)
                            nc.gpsimd.memset(w_lo[:, U_GATE % 4, :, :].bitcast(F32), 0.0).then_inc(gate_slots_zeroed, 1)

                groups(pool, u_base + 2 * FT, 4 * DT, 8, down)

            link(nc.gpsimd.memset(sq_sum[:, :], 0.0))
            for n, c in enumerate(X_ORDER):
                r = P if c < NC else TS
                pool.wait_ge(x_summed, n + 1)
                nc.gpsimd.tensor_scalar(sq_sum[0:r, CH[c]], ident[0:r, 0:r], x_sums[0:r, c:c + 1], None, ALU.mult)\
                    .then_inc(x_sums_spread, 1)
                if c == 2:
                    pool.wait_ge(w_hi_ready, 1)
                    nc.gpsimd.tensor_tensor(w_lo[:, 0, :, :], w_raw[:, 0, :, :], w_hi[:, 0, :, :].bitcast(F32), ALU.subtract)\
                        .then_inc(w_lo_ready, 1)
            ffn(0, U_F1, 0)

            pool.wait_ge(unit_done, U_GATE)
            link(nc.gpsimd.memset(mask[:, :], 0.0))
            link(triangle(mask[:, :], [[1, P]], ALU.is_ge, -1e30, mult=-1))
            link(nc.gpsimd.memset(sel[:, :, :], 1.0))
            link(triangle(sel[:, :, :], [[-1, H], [0, P]], ALU.is_equal, 0.0))
            nc.gpsimd.memset(row_cols[:, :], 0.0)
            nc.gpsimd.memset(neg_m_exp[:, :, :], 1.0)
            nc.gpsimd.memset(v_tok[:, :, P:V1], 1.0)
            nc.gpsimd.memset(small[:, 0, :], 1.0)
            nc.gpsimd.memset(mean_var[:, :, :], 0.0)
            nc.gpsimd.memset(small[:, 6, :], -0.5)
            nc.gpsimd.memset(state_in[:, H:2 * H, P:V1], 0.0).then_inc(mixer_consts, 1)

            def step_q_past(h):
                if h < H:
                    pool.wait_ge(past_ready, h + 1)
                    pool.wait_ge(evicted, T_IN + 4 * h + 1)
                else:
                    pool.wait_ge(rotated, 2 * (h - H) + 1)
                if h:
                    pool.wait_ge(mixed_done, h)
                if h < H:
                    nc.gpsimd.tensor_tensor(q_past[:, :], proj[:, h % 2, 0, :], past[:, :], ALU.mult).then_inc(q_past_ready, 1)
                    return
                grid = lambda ap: ap.rearrange("p (c d) -> p c d", c=NC)
                d = CROSS + (h - H) * P
                cross = table[:, d:d + P].rearrange("p (c d) -> p c d", c=1).broadcast_to([P, NC, P])
                nc.gpsimd.tensor_tensor(grid(q_past[:, 0:TP]), grid(proj[:, h % 2, 0, 0:TP]), cross, ALU.mult)
                nc.gpsimd.tensor_tensor(q_past[:, TP:T], proj[:, h % 2, 0, TP:T], table[:, d:d + TS], ALU.mult)\
                    .then_inc(q_past_ready, 1)

            def step_root(h):
                pool.wait_ge(var_ready, h + 1)
                nc.gpsimd.tensor_tensor(small[:, 3, :], small[:, 2, :], small[:, 6, :], ALU.pow).then_inc(root_ready, 1)

            def step_y_lo(h):
                pool.wait_ge(y_hi_ready, h + 1)
                nc.gpsimd.tensor_tensor(y_lo(h), y_f[:, :], y_hi(h).bitcast(F32), ALU.subtract).then_inc(y_lo_ready, 1)

            for h in range(2 * H):
                for u in range(4):
                    if h >= H and u < 2:
                        pool.wait_ge(evicted, T_IN + 4 * h + u + 1)
                        nc.gpsimd.tensor_tensor(proj[:, h % 2, u, :], rot[:, 0, :], rot[:, 1, :], ALU.add).then_inc(rotated, 1)
                    if h == 1 and u == 3:
                        pool.wait_ge(table_loaded, 16)
                        pool.wait_ge(rstd_ready, 2)
                        nc.gpsimd.tensor_tensor(table[:, COS:COS + T], table[:, COS:COS + T], rstd[:, :], ALU.mult)
                        nc.gpsimd.tensor_tensor(table[:, SIN:SIN + T], table[:, SIN:SIN + T], rstd[:, :], ALU.mult)\
                            .then_inc(tables_scaled, 1)
                    if h and u == 1:
                        step_root(h - 1)
                    if u == 2:
                        if h:
                            step_y_lo(h - 1)
                        step_q_past(h)
            step_root(2 * H - 1)
            for j in range(DT):
                add_square(0, j, 2, 0, reset=j == 0)

            ffn(1, U_F2, 2)


_INS = ['x_prompt', 'x_sample', 'state_mlstm_C', 'state_mlstm_n', 'state_mlstm_m', 'state_ret_R', 'g_ffn1',
        'w_ffn1_gate', 'w_ffn1_up', 'w_ffn1_down', 'g_mix', 'w_in', 'b_gates', 'g_gn_mlstm', 'g_gn_ret', 'w_out',
        'g_ffn2', 'w_ffn2_gate', 'w_ffn2_up', 'w_ffn2_down', 'g_final']


def kernel(**inputs):
    import numpy as _np
    import concourse.bacc as _bacc
    from concourse import mybir as _mybir
    from concourse.bass_utils import run_bass_kernel_spmd as _run

    xp, xs = inputs['x_prompt'].shape, inputs['x_sample'].shape
    state, norm = (1, 1, H, P, P), (1, 1, H, P)
    outs = [xp, xs] + 2 * [state, norm, (1, 1, H), state]
    nc = _bacc.Bacc("TRN2", target_bir_lowering=False, num_devices=1)
    arrays, args = {}, []
    for name in _INS:
        arrays[f"in_{name}"] = _np.ascontiguousarray(inputs[name])
    arrays["in_tables"] = shape_tables(xp[1], xs[1])
    for name, a in arrays.items():
        args.append(nc.dram_tensor(name, a.shape, _mybir.dt.from_np(a.dtype), kind="ExternalInput").ap())
    for i, shape in enumerate(outs):
        args.append(nc.dram_tensor(f"out_{i}", shape, _mybir.dt.float32, kind="ExternalOutput").ap())
    hybrid_trunk_step(nc, *args)
    r = _run(nc, [arrays], core_ids=[0])
    return tuple(r.results[0][f"out_{i}"] for i in range(len(outs)))
```
